# Optimizing a Trainium2 kernel written in Bass

```python
import math
import jax, jax.numpy as jnp
from jax import lax
import numpy as np

D_MODEL = 1024
BATCH = 1
SEQ = 256
DEPTH = 2

CHUNK = 64
HEAD_DIM = 64
D_POOL = D_MODEL // 4
POOL_WINDOWS = (2, 4, 8, 16)
N_POOL_GROUPS = len(POOL_WINDOWS)
POOL_GROUP = D_POOL // N_POOL_GROUPS
D_CHUNK = 3 * D_MODEL // 8
N_CHUNK_HEADS = D_CHUNK // HEAD_DIM
LEFT_CHUNKS = 8
BAND = (LEFT_CHUNKS + 1) * CHUNK
REL_CLIP = 128
D_SB = D_MODEL - D_POOL - D_CHUNK
N_SB_HEADS = D_SB // HEAD_DIM
SB_BLOCK = 128
D_IN = D_POOL + 3 * D_CHUNK + 3 * D_SB
D_FF = ((8 * D_MODEL // 3 + 127) // 128) * 128
N_EXPERTS = 8
TOP_K = 2
D_FF_EXPERT = D_FF
N_DENSE = (DEPTH + 1) // 2
N_MOE = DEPTH // 2
ALPHA = (2.0 * DEPTH) ** 0.25
BETA = (8.0 * DEPTH) ** -0.25
LN_EPS = 1e-5
RMS_EPS = 1e-6
NEG_INF = -1e30


def layer_norm(x, g, b):
    xf = x.astype(jnp.float32)
    mu = jnp.mean(xf, axis=-1, keepdims=True)
    xc = xf - mu
    var = jnp.mean(xc * xc, axis=-1, keepdims=True)
    y = xc * lax.rsqrt(var + LN_EPS) * g.astype(jnp.float32) + b.astype(jnp.float32)
    return y.astype(x.dtype)

def rms_normalise(y):
    yf = y.astype(jnp.float32)
    return yf * lax.rsqrt(jnp.mean(yf * yf, axis=-1, keepdims=True) + RMS_EPS)

def pool_mixer(u, pool_w, pool_scale):
    B, S, _ = u.shape
    uf = u.astype(jnp.float32)
    cs = jnp.cumsum(uf, axis=1)
    t = jnp.arange(S, dtype=jnp.float32)[None, :, None]
    outs = []
    for g, w in enumerate(POOL_WINDOWS):
        c = cs[..., g * POOL_GROUP:(g + 1) * POOL_GROUP]
        lag = jnp.pad(c[:, :-w], ((0, 0), (w, 0), (0, 0)))
        cnt = jnp.minimum(t + 1.0, float(w))
        outs.append((c - lag) / cnt)
    pooled = jnp.concatenate(outs, axis=-1) - uf
    pooled = pooled.reshape(B, S, N_POOL_GROUPS, POOL_GROUP)
    y = jnp.einsum('bsgc,gcd->bsgd', pooled, pool_w.astype(jnp.float32))
    return y.reshape(B, S, D_POOL) * pool_scale.astype(jnp.float32)

def chunk_attention(q, k, v, rel_bias):
    B, S, H, d = q.shape
    nc = S // CHUNK
    qc = q.reshape(B, nc, CHUNK, H, d).astype(jnp.float32)
    pad = ((0, 0), (LEFT_CHUNKS, 0), (0, 0), (0, 0), (0, 0))
    kc = jnp.pad(k.reshape(B, nc, CHUNK, H, d).astype(jnp.float32), pad)
    vc = jnp.pad(v.reshape(B, nc, CHUNK, H, d).astype(jnp.float32), pad)
    kband = jnp.concatenate([kc[:, j:j + nc] for j in range(LEFT_CHUNKS + 1)], axis=2)
    vband = jnp.concatenate([vc[:, j:j + nc] for j in range(LEFT_CHUNKS + 1)], axis=2)
    scores = jnp.einsum('bnqhd,bnkhd->bhnqk', qc, kband) * (1.0 / math.sqrt(d))
    qi = jnp.arange(CHUNK)[:, None]
    kj = jnp.arange(BAND)[None, :]
    rel = jnp.clip(qi + LEFT_CHUNKS * CHUNK - kj, -REL_CLIP, REL_CLIP) + REL_CLIP
    bias = rel_bias.astype(jnp.float32)[:, rel]
    key_chunk = jnp.arange(nc)[:, None] - LEFT_CHUNKS + jnp.arange(BAND)[None, :] // CHUNK
    valid = key_chunk >= 0
    scores = scores + bias[None, :, None, :, :]
    scores = jnp.where(valid[None, None, :, None, :], scores, NEG_INF)
    p = jax.nn.softmax(scores, axis=-1)
    o = jnp.einsum('bhnqk,bnkhd->bnqhd', p, vband)
    return o.reshape(B, S, H * d)

def stick_breaking_attention(q, k, v):
    B, S, H, d = q.shape
    qh = q.transpose(0, 2, 1, 3).astype(jnp.float32)
    kh = k.transpose(0, 2, 1, 3).astype(jnp.float32)
    vh = v.transpose(0, 2, 1, 3).astype(jnp.float32)
    scale = 1.0 / math.sqrt(d)
    outs = []
    for blk in range(S // SB_BLOCK):
        lo = blk * SB_BLOCK
        hi = lo + SB_BLOCK
        z = jnp.einsum('bhqd,bhkd->bhqk', qh[:, :, lo:hi], kh[:, :, :hi]) * scale
        t = lo + jnp.arange(SB_BLOCK)[:, None]
        s = jnp.arange(hi)[None, :]
        before = s < t
        log_keep = jnp.where(before, jax.nn.log_sigmoid(-z), 0.0)
        suffix = lax.cumsum(log_keep, axis=3, reverse=True) - log_keep
        w = jnp.where(before, jnp.exp(jax.nn.log_sigmoid(z) + suffix), 0.0)
        outs.append(jnp.einsum('bhqk,bhkd->bhqd', w, vh[:, :, :hi]))
    o = jnp.concatenate(outs, axis=2)
    return o.transpose(0, 2, 1, 3).reshape(B, S, H * d)

def hybrid_mixer(x, w_in, pool_w, pool_scale, rel_bias, g_mix, w_out):
    B, S, _ = x.shape
    h = x @ w_in
    u_pool = h[..., :D_POOL]
    qkv_c = h[..., D_POOL:D_POOL + 3 * D_CHUNK]
    qkv_s = h[..., D_POOL + 3 * D_CHUNK:]
    y_pool = pool_mixer(u_pool, pool_w, pool_scale)
    qc, kc, vc = [a.reshape(B, S, N_CHUNK_HEADS, HEAD_DIM) for a in jnp.split(qkv_c, 3, axis=-1)]
    y_chunk = chunk_attention(qc, kc, vc, rel_bias)
    qs, ks, vs = [a.reshape(B, S, N_SB_HEADS, HEAD_DIM) for a in jnp.split(qkv_s, 3, axis=-1)]
    y_sb = stick_breaking_attention(qs, ks, vs)
    y = jnp.concatenate([rms_normalise(y_pool), rms_normalise(y_chunk), rms_normalise(y_sb)], axis=-1)
    y = (y * g_mix.astype(jnp.float32)).astype(x.dtype)
    return y @ w_out

def swiglu(x, wg, wu, wd):
    return (jax.nn.silu(x @ wg) * (x @ wu)) @ wd

def moe_swiglu(x, router, wg, wu, wd):
    B, S, D = x.shape
    xt = x.reshape(B * S, D)
    logits = (xt @ router).astype(jnp.float32)
    top_val, top_idx = lax.top_k(logits, TOP_K)
    top_w = jax.nn.softmax(top_val, axis=-1)
    gates = jnp.sum(jax.nn.one_hot(top_idx, N_EXPERTS, dtype=jnp.float32) * top_w[..., None], axis=1)
    out = jnp.zeros((B * S, D), jnp.float32)
    for e in range(N_EXPERTS):
        out = out + gates[:, e:e + 1] * swiglu(xt, wg[e], wu[e], wd[e]).astype(jnp.float32)
    return out.reshape(B, S, D).astype(x.dtype)

def first_inputs(seed: int = 0) -> dict:
    key = jax.random.key(seed)
    ks = jax.random.split(key, 20)
    f32 = jnp.float32
    n = lambda k, shape, s: jax.random.normal(k, shape, f32) * s
    x = jax.random.normal(ks[0], (BATCH, SEQ, D_MODEL), f32)
    w_in = n(ks[1], (DEPTH, D_MODEL, D_IN), D_MODEL ** -0.5)
    pool_w = n(ks[2], (DEPTH, N_POOL_GROUPS, POOL_GROUP, POOL_GROUP), POOL_GROUP ** -0.5)
    pool_scale = 1.0 + n(ks[3], (DEPTH, D_POOL), 0.05)
    rel_bias = n(ks[4], (DEPTH, N_CHUNK_HEADS, 2 * REL_CLIP + 1), 0.3)
    g_mix = 1.0 + n(ks[5], (DEPTH, D_MODEL), 0.05)
    w_out = n(ks[6], (DEPTH, D_MODEL, D_MODEL), BETA * D_MODEL ** -0.5)
    ln1_g = 1.0 + n(ks[7], (DEPTH, D_MODEL), 0.05)
    ln1_b = n(ks[8], (DEPTH, D_MODEL), 0.02)
    ln2_g = 1.0 + n(ks[9], (DEPTH, D_MODEL), 0.05)
    ln2_b = n(ks[10], (DEPTH, D_MODEL), 0.02)
    ffn_wg = n(ks[11], (N_DENSE, D_MODEL, D_FF), D_MODEL ** -0.5)
    ffn_wu = n(ks[12], (N_DENSE, D_MODEL, D_FF), D_MODEL ** -0.5)
    ffn_wd = n(ks[13], (N_DENSE, D_FF, D_MODEL), BETA * D_FF ** -0.5)
    moe_router = n(ks[14], (N_MOE, D_MODEL, N_EXPERTS), D_MODEL ** -0.5)
    moe_wg = n(ks[15], (N_MOE, N_EXPERTS, D_MODEL, D_FF_EXPERT), D_MODEL ** -0.5)
    moe_wu = n(ks[16], (N_MOE, N_EXPERTS, D_MODEL, D_FF_EXPERT), D_MODEL ** -0.5)
    moe_wd = n(ks[17], (N_MOE, N_EXPERTS, D_FF_EXPERT, D_MODEL), BETA * D_FF_EXPERT ** -0.5)
    return {"x": x, "w_in": w_in, "pool_w": pool_w, "pool_scale": pool_scale, "rel_bias": rel_bias,
            "g_mix": g_mix, "w_out": w_out, "ln1_g": ln1_g, "ln1_b": ln1_b, "ln2_g": ln2_g, "ln2_b": ln2_b,
            "ffn_wg": ffn_wg, "ffn_wu": ffn_wu, "ffn_wd": ffn_wd, "moe_router": moe_router,
            "moe_wg": moe_wg, "moe_wu": moe_wu, "moe_wd": moe_wd}

def first_block(x, w_in, pool_w, pool_scale, rel_bias, g_mix, w_out, ln1_g, ln1_b, ln2_g, ln2_b,
              ffn_wg, ffn_wu, ffn_wd, moe_router, moe_wg, moe_wu, moe_wd):
    for i in range(DEPTH):
        m = hybrid_mixer(x, w_in[i], pool_w[i], pool_scale[i], rel_bias[i], g_mix[i], w_out[i])
        x = layer_norm(ALPHA * x + m, ln1_g[i], ln1_b[i])
        j = i // 2
        if i % 2 == 0:
            f = swiglu(x, ffn_wg[j], ffn_wu[j], ffn_wd[j])
        else:
            f = moe_swiglu(x, moe_router[j], moe_wg[j], moe_wu[j], moe_wd[j])
        x = layer_norm(ALPHA * x + f, ln2_g[i], ln2_b[i])
    return x


GRID_W = 64
BLOCK = 128
NA_HEADS = 8
NA_ROW_K = 8
NA_COL_K = 16
SW_Q_HEADS = 8
SW_KV_HEADS = 2
SW_WINDOW = 128
DIFF_HEADS = 4
N_BRANCH = 3
BRANCH_W = 512
D_FF_2 = 2816
ROPE_THETA = 10000.0
EPS = 1e-6
NEG = -1e30

A_W = NA_HEADS * HEAD_DIM
B_QW = SW_Q_HEADS * HEAD_DIM
B_KVW = SW_KV_HEADS * HEAD_DIM
C_QKW = 2 * DIFF_HEADS * HEAD_DIM
C_VW = DIFF_HEADS * 2 * HEAD_DIM
SPLIT_SIZES = (A_W, A_W, A_W, B_QW, B_KVW, B_KVW, C_QKW, C_QKW, C_VW, N_BRANCH * D_MODEL)
IN_COLS = sum(SPLIT_SIZES)


def rmsnorm(x, g):
    xf = x.astype(jnp.float32)
    y = xf * lax.rsqrt(jnp.mean(xf * xf, axis=-1, keepdims=True) + EPS)
    return (y * g.astype(jnp.float32)).astype(x.dtype)

def swiglu_2(x, w_gu, w_down):
    gate, up = jnp.split(x @ w_gu, 2, axis=-1)
    return (jax.nn.silu(gate) * up) @ w_down

def rope_tables(s):
    pos = jnp.arange(s, dtype=jnp.float32)
    inv = ROPE_THETA ** (-jnp.arange(0, HEAD_DIM, 2, dtype=jnp.float32) / HEAD_DIM)
    ang = pos[:, None] * inv[None, :]
    ang = jnp.concatenate([ang, ang], axis=-1)
    return jnp.cos(ang), jnp.sin(ang)

def apply_rope(t, cos, sin):
    t1, t2 = jnp.split(t, 2, axis=-1)
    rot = jnp.concatenate([-t2, t1], axis=-1)
    return t * cos.astype(t.dtype) + rot * sin.astype(t.dtype)

def split_heads(t, n):
    b, s, _ = t.shape
    return t.reshape(b, s, n, HEAD_DIM).transpose(0, 2, 1, 3)

def neighbourhood_attention(q, k, v, rpb):
    b, h, s, d = q.shape
    rows = s // GRID_W
    kr = min(NA_ROW_K, rows)
    kc = NA_COL_K
    r = jnp.arange(rows)
    c = jnp.arange(GRID_W)
    row_start = jnp.clip(r - kr // 2, 0, rows - kr)
    col_start = jnp.clip(c - kc // 2, 0, GRID_W - kc)
    key_rows = row_start[:, None] + jnp.arange(kr)[None, :]
    qg = q.reshape(b, h, rows, GRID_W, d)
    kg = k.reshape(b, h, rows, GRID_W, d)[:, :, key_rows]
    vg = v.reshape(b, h, rows, GRID_W, d)[:, :, key_rows]
    scores = jnp.einsum('bhrcd,bhrijd->bhrcij', qg, kg).astype(jnp.float32) * (d ** -0.5)
    dr = key_rows - r[:, None] + (NA_ROW_K - 1)
    dc = jnp.clip(c[None, :] - c[:, None] + (NA_COL_K - 1), 0, 2 * NA_COL_K - 2)
    bias = rpb[:, dr[:, None, :, None], dc[None, :, None, :]]
    col_ok = (c[None, :] >= col_start[:, None]) & (c[None, :] < col_start[:, None] + kc)
    scores = scores + bias[None].astype(jnp.float32)
    scores = jnp.where(col_ok[None, None, None, :, None, :], scores, NEG)
    p = jax.nn.softmax(scores.reshape(b, h, rows, GRID_W, kr * GRID_W), axis=-1)
    p = p.reshape(b, h, rows, GRID_W, kr, GRID_W).astype(v.dtype)
    out = jnp.einsum('bhrcij,bhrijd->bhrcd', p, vg)
    return out.reshape(b, h, s, d)

def sliding_window_attention(q, k, v, sink):
    b, hq, s, d = q.shape
    hkv = k.shape[1]
    g = hq // hkv
    nb = s // BLOCK
    qb = q.reshape(b, hkv, g, nb, BLOCK, d)

    def band(t):
        tp = jnp.pad(t, ((0, 0), (0, 0), (BLOCK, BLOCK), (0, 0))).reshape(b, hkv, nb + 2, BLOCK, d)
        return jnp.concatenate([tp[:, :, :-2], tp[:, :, 1:-1], tp[:, :, 2:]], axis=3)

    kb, vb = band(k), band(v)
    scores = jnp.einsum('bkgnqd,bknjd->bkgnqj', qb, kb).astype(jnp.float32) * (d ** -0.5)
    qpos = jnp.arange(nb)[:, None] * BLOCK + jnp.arange(BLOCK)[None, :]
    kpos = (jnp.arange(nb)[:, None] - 1) * BLOCK + jnp.arange(3 * BLOCK)[None, :]
    ok = ((jnp.abs(qpos[:, :, None] - kpos[:, None, :]) <= SW_WINDOW)
          & (kpos[:, None, :] >= 0) & (kpos[:, None, :] < s))
    scores = jnp.where(ok, scores, NEG)
    sink_logit = jnp.broadcast_to(sink.astype(jnp.float32).reshape(1, hkv, g, 1, 1, 1),
                                  scores.shape[:-1] + (1,))
    p = jax.nn.softmax(jnp.concatenate([scores, sink_logit], axis=-1), axis=-1)[..., :-1]
    out = jnp.einsum('bkgnqj,bknjd->bkgnqd', p.astype(v.dtype), vb)
    return out.reshape(b, hq, s, d)

def differential_attention(q, k, v, lam, lam_init, subln_g):
    b, h, _, s, d = q.shape
    nb = s // BLOCK
    qb = jnp.moveaxis(q.reshape(b, h, 2, nb, BLOCK, d), 3, 0)

    def one_block(qblk):
        sc = jnp.einsum('bhtqd,bhtkd->bhtqk', qblk, k).astype(jnp.float32) * (d ** -0.5)
        p = jax.nn.softmax(sc, axis=-1)
        a = p[:, :, 0] - lam * p[:, :, 1]
        return jnp.einsum('bhqk,bhke->bhqe', a.astype(v.dtype), v)

    o = lax.map(one_block, qb)
    o = jnp.moveaxis(o, 0, 2).reshape(b, h, s, 2 * d)
    return rmsnorm(o, subln_g) * (1.0 - lam_init)

def second_inputs(seed: int = 0) -> dict:
    key = jax.random.key(seed)
    ks = jax.random.split(key, 24)
    L, D, F = DEPTH, D_MODEL, D_FF_2

    def nrm(k, shape, scale):
        return jax.random.normal(k, shape, jnp.float32) * scale

    def gain(k, n):
        return 1.0 + nrm(k, (L, n), 0.05)

    return {
        "x": nrm(ks[0], (BATCH, SEQ, D), 1.0),
        "ffn1_pre_g": gain(ks[1], D),
        "ffn1_w_gu": nrm(ks[2], (L, D, 2 * F), D ** -0.5),
        "ffn1_w_down": nrm(ks[3], (L, F, D), F ** -0.5),
        "ffn1_post_g": gain(ks[4], D),
        "mix_pre_g": gain(ks[5], D),
        "w_in": nrm(ks[6], (L, D, IN_COLS), D ** -0.5),
        "na_rpb": nrm(ks[7], (L, NA_HEADS, 2 * NA_ROW_K - 1, 2 * NA_COL_K - 1), 0.5),
        "sw_sink": nrm(ks[8], (L, SW_Q_HEADS), 1.0),
        "diff_lambda_q1": nrm(ks[9], (L, HEAD_DIM), 0.1),
        "diff_lambda_k1": nrm(ks[10], (L, HEAD_DIM), 0.1),
        "diff_lambda_q2": nrm(ks[11], (L, HEAD_DIM), 0.1),
        "diff_lambda_k2": nrm(ks[12], (L, HEAD_DIM), 0.1),
        "diff_subln_g": gain(ks[13], 2 * HEAD_DIM),
        "w_branch": nrm(ks[14], (L, N_BRANCH, BRANCH_W, D), BRANCH_W ** -0.5),
        "b_gate": nrm(ks[15], (L, N_BRANCH, D), 0.1),
        "w_out": nrm(ks[16], (L, D, D), D ** -0.5),
        "mix_post_g": gain(ks[17], D),
        "ffn2_pre_g": gain(ks[18], D),
        "ffn2_w_gu": nrm(ks[19], (L, D, 2 * F), D ** -0.5),
        "ffn2_w_down": nrm(ks[20], (L, F, D), F ** -0.5),
        "ffn2_post_g": gain(ks[21], D),
    }

def second_block(x, ffn1_pre_g, ffn1_w_gu, ffn1_w_down, ffn1_post_g, mix_pre_g, w_in, na_rpb,
              sw_sink, diff_lambda_q1, diff_lambda_k1, diff_lambda_q2, diff_lambda_k2,
              diff_subln_g, w_branch, b_gate, w_out, mix_post_g, ffn2_pre_g, ffn2_w_gu,
              ffn2_w_down, ffn2_post_g):
    b, s, _ = x.shape
    cos, sin = rope_tables(s)
    split_at = np.cumsum(SPLIT_SIZES)[:-1].tolist()
    h = x
    for l in range(DEPTH):
        y = swiglu_2(rmsnorm(h, ffn1_pre_g[l]), ffn1_w_gu[l], ffn1_w_down[l])
        h = h + 0.5 * rmsnorm(y, ffn1_post_g[l])

        u = rmsnorm(h, mix_pre_g[l])
        proj = u @ w_in[l]
        qa, ka, va, qb, kb, vb, qc, kc, vc, gl = jnp.split(proj, split_at, axis=-1)

        oa = neighbourhood_attention(split_heads(qa, NA_HEADS), split_heads(ka, NA_HEADS),
                                     split_heads(va, NA_HEADS), na_rpb[l])
        oa = oa.transpose(0, 2, 1, 3).reshape(b, s, A_W)

        ob = sliding_window_attention(apply_rope(split_heads(qb, SW_Q_HEADS), cos, sin),
                                      apply_rope(split_heads(kb, SW_KV_HEADS), cos, sin),
                                      split_heads(vb, SW_KV_HEADS), sw_sink[l])
        ob = ob.transpose(0, 2, 1, 3).reshape(b, s, B_QW)

        qc = apply_rope(qc.reshape(b, s, DIFF_HEADS, 2, HEAD_DIM).transpose(0, 2, 3, 1, 4), cos, sin)
        kc = apply_rope(kc.reshape(b, s, DIFF_HEADS, 2, HEAD_DIM).transpose(0, 2, 3, 1, 4), cos, sin)
        vc = vc.reshape(b, s, DIFF_HEADS, 2 * HEAD_DIM).transpose(0, 2, 1, 3)
        lam_init = 0.8 - 0.6 * math.exp(-0.3 * l)
        lam = (jnp.exp(jnp.sum(diff_lambda_q1[l].astype(jnp.float32) * diff_lambda_k1[l].astype(jnp.float32)))
               - jnp.exp(jnp.sum(diff_lambda_q2[l].astype(jnp.float32) * diff_lambda_k2[l].astype(jnp.float32)))
               + lam_init)
        oc = differential_attention(qc, kc, vc, lam, lam_init, diff_subln_g[l])
        oc = oc.transpose(0, 2, 1, 3).reshape(b, s, C_VW)

        branches = jnp.stack([oa, ob, oc], axis=2)
        yb = jnp.einsum('bsnc,ncd->bsnd', branches, w_branch[l])
        gates = jax.nn.sigmoid(gl.reshape(b, s, N_BRANCH, D_MODEL) + b_gate[l])
        merged = jnp.sum(gates * yb, axis=2)
        h = h + rmsnorm(merged @ w_out[l], mix_post_g[l])

        y = swiglu_2(rmsnorm(h, ffn2_pre_g[l]), ffn2_w_gu[l], ffn2_w_down[l])
        h = h + 0.5 * rmsnorm(y, ffn2_post_g[l])
    return h


def setup_inputs(seed=0):
    out = dict(first_inputs(seed))
    for name, value in second_inputs(seed + 1).items():
        if name != "x":
            out[name + "_2"] = value
    return out


def reference(
    x, w_in, pool_w, pool_scale, rel_bias, g_mix, w_out, ln1_g, ln1_b, ln2_g, ln2_b, ffn_wg,
    ffn_wu, ffn_wd, moe_router, moe_wg, moe_wu, moe_wd, ffn1_pre_g_2, ffn1_w_gu_2,
    ffn1_w_down_2, ffn1_post_g_2, mix_pre_g_2, w_in_2, na_rpb_2, sw_sink_2, diff_lambda_q1_2,
    diff_lambda_k1_2, diff_lambda_q2_2, diff_lambda_k2_2, diff_subln_g_2, w_branch_2, b_gate_2,
    w_out_2, mix_post_g_2, ffn2_pre_g_2, ffn2_w_gu_2, ffn2_w_down_2, ffn2_post_g_2,
):
    x = first_block(
        x, w_in, pool_w, pool_scale, rel_bias, g_mix, w_out, ln1_g, ln1_b, ln2_g, ln2_b, ffn_wg,
        ffn_wu, ffn_wd, moe_router, moe_wg, moe_wu, moe_wd,
    )
    return second_block(
        x, ffn1_pre_g_2, ffn1_w_gu_2, ffn1_w_down_2, ffn1_post_g_2, mix_pre_g_2, w_in_2,
        na_rpb_2, sw_sink_2, diff_lambda_q1_2, diff_lambda_k1_2, diff_lambda_q2_2,
        diff_lambda_k2_2, diff_subln_g_2, w_branch_2, b_gate_2, w_out_2, mix_post_g_2,
        ffn2_pre_g_2, ffn2_w_gu_2, ffn2_w_down_2, ffn2_post_g_2,
    )


_drawn_inputs = setup_inputs


def setup_inputs(seed=0):
    import zlib

    import numpy as np

    out = dict(_drawn_inputs(seed))
    spreads = {}
    factors = {'pool_scale': 3.155, 'sw_sink_2': 8.0, 'diff_lambda_k1_2': 4.998, 'ffn2_post_g_2': 2.706}
    for name, (base, spread) in spreads.items():
        noise = np.random.default_rng([zlib.crc32(name.encode()), seed]).standard_normal(out[name].shape)
        drawn = base * np.exp(spread * noise) if base else spread * noise
        out[name] = __import__('jax').numpy.asarray(drawn.astype(out[name].dtype))
    for name, factor in factors.items():
        out[name] = (out[name] * factor).astype(out[name].dtype)
    return out
```

```python
import math
from contextlib import ExitStack

import numpy as np

import concourse.bass as bass
from concourse import mybir

F32 = mybir.dt.float32
F32R = mybir.dt.float32r
BF16 = mybir.dt.bfloat16
ALU = mybir.AluOpType
ACT = mybir.ActivationFunctionType
AX_X = mybir.AxisListType.X

P = 128
D = 1024
S = 256
TT = S // P
KD = D // P
HD = 64
N_LAYERS = 2
FF = 2816
FCH = 256
N_FCH = FF // FCH
N_EXPERTS = 8
CHUNK_HEADS = 6
SB_HEADS = 6
NA_HEADS = 8
SW_HEADS = 8
DIFF_HEADS = 4
D_POOL = 256
D_CHUNK = 384
D_SB = 384
D_IN = 2560
REL_CLIP = 128
NA_ROWS = 4
GRID_W = 64
ALPHA = (2.0 * N_LAYERS) ** 0.25
LN_EPS = 1e-5
RMS_EPS = 1e-6
NEG = -1e30
SCALE = 1.0 / math.sqrt(HD)
POOL_WINDOWS = (2, 4, 8, 16)

QA, KA, VA, QB, KB, QC, KC, VC, GL = 0, 512, 1024, 1536, 2048, 2304, 2816, 3328, 3840


def shape_constants():
    q = np.arange(S)[:, None]
    k = np.arange(S)[None, :]
    chunk_mask = np.where(k // 64 <= q // 64, 0.0, NEG)[:, ::-1]
    sb_mask = np.where(k < q, 0.0, NEG)
    sw_mask = np.where(np.abs(q - k) <= 128, 0.0, NEG)
    c0 = np.clip(q % GRID_W - 8, 0, GRID_W - 16)
    na_mask = np.where((k % GRID_W >= c0) & (k % GRID_W < c0 + 16), 0.0, NEG)[:, ::-1]
    masks = np.stack([chunk_mask, sb_mask, na_mask, sw_mask]).astype(np.float32)
    pos = np.arange(S, dtype=np.float32)
    inv = np.float32(10000.0) ** (-np.arange(0, HD, 2, dtype=np.float32) / np.float32(HD))
    ang = (pos[:, None] * inv[None, :]).astype(np.float32)
    ang = np.concatenate([ang, ang], axis=1)
    sign = np.concatenate([-np.ones(32), np.ones(32)])[None, :]
    rope = np.stack([np.cos(ang), np.sin(ang) * sign]).astype(np.float32)
    pool = np.zeros((S, 4, S), np.float64)
    for g, w in enumerate(POOL_WINDOWS):
        for t in range(S):
            lo = max(0, t - w + 1)
            pool[lo:t + 1, g, t] += 1.0 / min(t + 1, w)
            pool[t, g, t] -= 1.0
    earlier = np.broadcast_to(np.tril(np.ones((8, 8)), -1).reshape(1, 64), (P, 64))
    return {"c_masks": masks, "c_rope": rope, "c_pool": pool.astype(np.float32),
            "c_ident": np.eye(P, dtype=np.float32), "c_earlier": np.ascontiguousarray(earlier, dtype=np.float32)}


class Chunk:

    def __init__(self, half, rest):
        self.half, self.rest = half, rest

    def at(self, base):
        return self.half * 2 + (self.rest + base)

    def turns(self, first):
        return self.half + (self.rest // 2 + first)

    def next(self, n=1):
        return Chunk(self.half, self.rest + n)


class Tally(dict):

    def __missing__(self, key):
        return 0


def program(nc, a, out):
    with ExitStack() as ctx:
        def sb(name, shape, dt=F32):
            return ctx.enter_context(nc.sbuf_tensor(name, shape, dt))

        def sem(name):
            return ctx.enter_context(nc.semaphore(name))

        raw_a = sb("raw_a", [P, 2, 4096])
        hi_a = sb("hi_a", [P, 2, 4096], F32R)
        lo_a = sb("lo_a", [P, 2, 4096], F32R)
        raw_b = sb("raw_b", [P, 2048])
        hi_b = sb("hi_b", [P, 2048], F32R)
        lo_b = sb("lo_b", [P, 2048], F32R)
        x = sb("x", [P, TT, D])
        t = sb("t", [P, TT, D])
        uT_hi = sb("uT_hi", [P, KD, S], F32R)
        uT_lo = sb("uT_lo", [P, KD, S], F32R)
        hT_hi = sb("hT_hi", [P, 4, S], F32R)
        hT_lo = sb("hT_lo", [P, 4, S], F32R)
        rows = sb("rows", [P, TT, D_IN])
        merged = sb("merged", [P, TT, D])
        vec = sb("vec", [P, 2, D])
        qkT = sb("qkT", [P, 2, 512])
        sc = sb("sc", [P, 2, TT, S])
        pT = sb("pT", [P, 2, TT, S])
        bias = sb("bias", [P, 2, TT, S])
        mask = sb("mask", [P, TT, S])
        ident = sb("ident", [P, P])
        rope = sb("rope", [P, 2, TT, HD])
        zeros = sb("zeros", [P, 512], BF16)
        stat = sb("stat", [P, 256])
        earlier = sb("earlier", [P, 64])
        rt = sb("rt", [P, 64])
        rt_hi = sb("rt_hi", [P, 64], F32R)
        rt_lo = sb("rt_lo", [P, 64], F32R)
        cmp1 = sb("cmp1", [P, 64])
        cmp2 = sb("cmp2", [P, 64])
        lam4 = sb("lam4", [P, 4, 64])
        pool_w = lam4[0:64, :, :]
        sink = sb("sink", [P, 8])

        ss = stat[:, 0:8]
        rstd = stat[:, 8:16]
        sm = stat[:, 16:18]
        nmean = stat[:, 18:20]
        half_pow = stat[:, 20:28]
        negmax = stat[:, 32:40].rearrange("p (s t) -> p s t", t=TT)
        psums = stat[:, 40:48].rearrange("p (s t) -> p s t", t=TT)
        esink = stat[:, 48:56].rearrange("p (s t) -> p s t", t=TT)
        rsum = stat[:, 56:64].rearrange("p (s t) -> p s t", t=TT)
        logit = stat[:, 64:80].rearrange("p (t e) -> p t e", t=TT)
        top = stat[:, 80:82]
        rank = stat[:, 96:104]
        gates = stat[:, 104:120].rearrange("p (t e) -> p t e", t=TT)
        gsum = stat[:, 120:122]
        lam_s = stat[:, 124:126]
        lam_e = stat[:, 126:128]
        nlam = stat[:, 128:129]
        nsink = stat[:, 136:144]
        zcol = stat[:, 144:145]

        acc = ctx.enter_context(nc.psum_tensor("acc", [P, 4, 512], F32))
        pp = ctx.enter_context(nc.psum_tensor("pp", [P, TT, 512], F32))
        tp = ctx.enter_context(nc.psum_tensor("tp", [P, 2, 512], F32))

        ext1 = nc.dram_tensor("chunk_bias_rows", [12, 511], F32, kind="Internal").ap()
        ext2 = nc.dram_tensor("na_bias_rows", [112, 127], F32, kind="Internal").ap()

        s_const = sem("s_const")
        s_zero = sem("s_zero")
        s_xin = sem("s_xin")
        s_al = [sem("s_al0"), sem("s_al1")]
        s_bl = sem("s_bl")
        s_ahi = sem("s_ahi")
        s_alo = sem("s_alo")
        s_aused = sem("s_aused")
        s_bhi = sem("s_bhi")
        s_blo = sem("s_blo")
        s_bused = sem("s_bused")
        s_pp = sem("s_pp")
        s_ppa = sem("s_ppa")
        s_ppv = sem("s_ppv")
        s_acc = sem("s_acc")
        s_accfree = sem("s_accfree")
        s_tps = sem("s_tps")
        s_thi = sem("s_thi")
        s_tlo = sem("s_tlo")
        s_qkT = sem("s_qkT")
        s_rows = sem("s_rows")
        s_x = sem("s_x")
        s_sum = sem("s_sum")
        s_nmean = sem("s_nmean")
        s_ss = sem("s_ss")
        s_rstd = sem("s_rstd")
        s_vec = [sem("s_vec0"), sem("s_vec1")]
        s_vecused = sem("s_vecused")
        s_dve = sem("s_dve")
        s_pool = sem("s_pool")
        s_qk = sem("s_qk")
        s_sc = sem("s_sc")
        s_nm = sem("s_nm")
        s_ln = sem("s_ln")
        s_exp = sem("s_exp")
        s_comb = sem("s_comb")
        s_pt = sem("s_pt")
        s_pte = sem("s_pte")
        s_pv = sem("s_pv")
        s_o = sem("s_o")
        s_biasl = [sem("s_biasl0"), sem("s_biasl1")]
        s_bias = sem("s_bias")
        s_biasused = sem("s_biasused")
        s_mask = sem("s_mask")
        s_maskused = sem("s_maskused")
        s_ext = sem("s_ext")
        s_pw = sem("s_pw")
        s_pla = sem("s_pla")
        s_plb = sem("s_plb")
        s_plc = sem("s_plc")
        s_plo = sem("s_plo")
        s_rt = sem("s_rt")
        s_rhi = sem("s_rhi")
        s_rlo = sem("s_rlo")
        s_rex = sem("s_rex")
        s_rnt = sem("s_rnt")
        s_lam = sem("s_lam")
        s_lamv = sem("s_lamv")
        s_lame = sem("s_lame")
        s_merge = sem("s_merge")
        s_out = sem("s_out")

        def row_bcast(ap1d):
            return ap1d.unsqueeze(0).to_broadcast([P, ap1d.shape[0]])

        def gain_rows():
            seq = []
            for i in range(N_LAYERS):
                seq += [a["pool_scale"][i], a["g_mix"][i], a["ln1_g"][i], a["ln1_b"][i], a["ln2_g"][i], a["ln2_b"][i]]
            for l in range(N_LAYERS):
                seq += [a["ffn1_pre_g_2"][l], a["ffn1_post_g_2"][l], a["mix_pre_g_2"][l]]
                seq += [a["b_gate_2"][l, 0], a["b_gate_2"][l, 1], a["diff_subln_g_2"][l], a["b_gate_2"][l, 2]]
                seq += [a["mix_post_g_2"][l], a["ffn2_pre_g_2"][l], a["ffn2_post_g_2"][l]]
            return seq

        GAINS = gain_rows()
        block = ctx.enter_context(nc.Block())

        def wide(w, cols, n=512):
            return w.rearrange("(k p) n -> p k n", p=P)[:, :, cols:cols + n]

        def ffn_walk(eng, experts, a_side, b_side, head, tail, final=False):
            head()
            if experts == 1:
                turns = (N_FCH - 1) // 2 - final
                with eng.Fori(0, turns) as i:
                    for r in range(2):
                        both(a_side, b_side, Chunk(i, r), 0, i * 2 + (r + 1), 0, i * 2 + r)
                if final:
                    for r in range(2):
                        both(a_side, b_side, Chunk(turns, r), 0, turns * 2 + r + 1, 0, turns * 2 + r)
                tail(Chunk((N_FCH - 1) // 2, 0), 0, N_FCH - 1)
                return

            def pair(ep, last):
                base = ep * N_FCH
                with eng.Fori(0, (N_FCH - 1) // 2) as i:
                    for r in range(2):
                        both(a_side, b_side, Chunk(i + base, r), ep * 2, i * 2 + (r + 1), ep * 2, i * 2 + r)
                both(a_side, b_side, Chunk(base + 5, 0), ep * 2 + 1, 0, ep * 2, N_FCH - 1)
                with eng.Fori(0, (N_FCH - 1) // 2) as i:
                    for r in range(2):
                        both(a_side, b_side, Chunk(i + base + 5, 1 + r), ep * 2 + 1, i * 2 + (r + 1),
                             ep * 2 + 1, i * 2 + r)
                if not last:
                    both(a_side, b_side, Chunk(base + 10, 1), ep * 2 + 2, 0, ep * 2 + 1, N_FCH - 1)

            with eng.Fori(0, experts // 2 - 1) as ep:
                pair(ep, False)
            pair(experts // 2 - 1, True)
            tail(Chunk((experts // 2) * N_FCH - 1, 1), experts - 1, N_FCH - 1)

        def both(a_side, b_side, c, ea, ja, eb, jb):
            a_side(c.next(), ea, ja)
            b_side(c, eb, jb)

        @block.sync
        def _(sp):
            n = Tally()
            sp.dma_start(x[:, :, :], a["x"][0].rearrange("(t p) d -> p t d", p=P)).then_inc(s_xin, 16)

            n["b"] = 1

            def weight(src, k, cols):
                slot = n["a"] % 2
                if n["a"] >= 2:
                    sp.wait_ge(s_alo, n["a"] - 1)
                dst = raw_a[:, slot, 0:k * cols].rearrange("p (k n) -> p k n", k=k)
                for j in range(2):
                    sp.dma_start(dst[:, j * k // 2:(j + 1) * k // 2, :], src[:, j * k // 2:(j + 1) * k // 2, :]) \
                      .then_inc(s_al[slot], 16)
                n["a"] += 1

            def ffn(wg, wu, wd, experts, f0g, f0u):
                a0, b0 = n["a"], n["b"]

                def side_a(c, e, j):
                    slot = (a0 + c.rest) % 2
                    sp.wait_ge(s_alo, c.at(a0 - 1))
                    for g, (w, f0) in enumerate(((wg, f0g), (wu, f0u))):
                        v = w[bass.ds(e * D, D), bass.ds(j * FCH + f0, FCH)]
                        sp.dma_start(raw_a[:, slot, g * 2048:(g + 1) * 2048].rearrange("p (k n) -> p k n", k=KD),
                                     v.rearrange("(k p) n -> p k n", p=P)).then_inc(s_al[slot], 16)

                def side_b(c, e, j):
                    sp.wait_ge(s_blo, c.at(b0))
                    v = wd[bass.ds(e * FF + j * FCH, FCH), :]
                    sp.dma_start(raw_b[:, :].rearrange("p (k n) -> p k n", k=2),
                                 v.rearrange("(k p) n -> p k n", p=P)).then_inc(s_bl, 16)

                ffn_walk(sp, experts, side_a, side_b, lambda: side_a(Chunk(0, 0), 0, 0), side_b)
                n["a"] += experts * N_FCH
                n["b"] += experts * N_FCH

            for i in range(N_LAYERS):
                for j in range(D_IN // 512):
                    weight(wide(a["w_in"][i], 512 * j), KD, 512)
                for j in range(2):
                    weight(wide(a["w_out"][i], 512 * j), KD, 512)
                if i == 0:
                    ffn(a["ffn_wg"][0], a["ffn_wu"][0], a["ffn_wd"][0], 1, 0, 0)
                else:
                    ffn(a["moe_wg"][0].rearrange("e d f -> (e d) f"), a["moe_wu"][0].rearrange("e d f -> (e d) f"),
                        a["moe_wd"][0].rearrange("e f d -> (e f) d"), N_EXPERTS, 0, 0)
            for l in range(N_LAYERS):
                ffn(a["ffn1_w_gu_2"][l], a["ffn1_w_gu_2"][l], a["ffn1_w_down_2"][l], 1, 0, FF)
                w = a["w_in_2"][l]
                for br, cols in enumerate((((QA, 512), (KA, 512), (VA, 512)), ((QB, 512), (KB, 256)),
                                           ((QC, 512), (KC, 512), (VC, 512)))):
                    for c0, width in cols:
                        weight(wide(w, c0, width), KD, width)
                    for j in range(2):
                        weight(wide(w, GL + 1024 * br + 512 * j), KD, 512)
                    weight(a["w_branch_2"][l, br].rearrange("(k p) n -> p k n", p=P), 4, 1024)
                for j in range(2):
                    weight(wide(a["w_out_2"][l], 512 * j), KD, 512)
                ffn(a["ffn2_w_gu_2"][l], a["ffn2_w_gu_2"][l], a["ffn2_w_down_2"][l], 1, 0, FF)
            sp.wait_ge(s_x, 2 * N_LAYERS + 3 * N_LAYERS)
            sp.dma_start(out[0].rearrange("(t p) d -> p t d", p=P), x[:, :, :]).then_inc(s_out, 16)
            sp.wait_ge(s_out, 16)

        @block.tensor
        def _(pe):
            n = Tally()
            bank_free = [None, None]

            def split3(out_ap, l_hi, l_lo, r_hi, r_lo, start, stop):
                nc.tensor.matmul(out_ap, l_hi, r_hi, start=start, stop=False, skip_group_check=True)
                nc.tensor.matmul(out_ap, l_hi, r_lo, start=False, stop=False, skip_group_check=True)
                return nc.tensor.matmul(out_ap, l_lo, r_hi, start=False, stop=stop, skip_group_check=True)

            def group(srcs, value):
                bank = n["g"] % 2
                if bank_free[bank] is not None:
                    pe.wait_ge(*bank_free[bank])
                for dst, src in srcs:
                    mm = nc.tensor.transpose(tp[:, bank, dst:dst + P], src, ident[:, :])
                mm.then_inc(s_tps, 1)
                bank_free[bank] = value
                n["g"] += 1

            def transpose_rows(src, kt):
                n["rows"] += 1
                pe.wait_ge(s_rows, n["rows"])
                for g in range(kt // 2):
                    n["lo"] += 1
                    group([(kk * S + tt * P, src[:, tt, (2 * g + kk) * P:(2 * g + kk + 1) * P])
                           for kk in range(2) for tt in range(TT)], (s_tlo, n["lo"]))

            def wait_uT():
                pe.wait_ge(s_tlo, n["lo"])

            def take_a():
                n["a"] += 1
                pe.wait_ge(s_alo, n["a"])
                return (n["a"] - 1) % 2

            def wait_pp():
                if n["ppa"]:
                    pe.wait_ge(s_ppa, n["ppa"])
                if n["ppv"]:
                    pe.wait_ge(s_ppv, n["ppv"])

            def project(width=512):
                slot = take_a()
                wait_pp()
                wh = hi_a[:, slot, 0:KD * width].rearrange("p (k n) -> p k n", k=KD)
                wl = lo_a[:, slot, 0:KD * width].rearrange("p (k n) -> p k n", k=KD)
                for tt in range(TT):
                    for k in range(KD):
                        ts = slice(tt * P, (tt + 1) * P)
                        mm = split3(pp[:, tt, 0:width], uT_hi[:, k, ts], uT_lo[:, k, ts], wh[:, k, :], wl[:, k, :],
                                    k == 0, k == KD - 1)
                    mm.then_inc(s_pp, 1)
                n["pp"] += 2
                n["ppa"] += 2
                n["ppv"] += 2

            def project_out(kt, width, left_hi, left_lo, chunks):
                pe.wait_ge(s_accfree, n["acc"]) if n["acc"] else None
                for j in range(chunks):
                    slot = take_a()
                    wh = hi_a[:, slot, 0:kt * width].rearrange("p (k n) -> p k n", k=kt)
                    wl = lo_a[:, slot, 0:kt * width].rearrange("p (k n) -> p k n", k=kt)
                    for tt in range(TT):
                        for h in range(width // 512):
                            for k in range(kt):
                                ts = slice(tt * P, (tt + 1) * P)
                                cs = slice(h * 512, (h + 1) * 512)
                                mm = split3(acc[:, tt * 2 + j + h, :], left_hi[:, k, ts], left_lo[:, k, ts],
                                            wh[:, k, cs], wl[:, k, cs], k == 0, k == kt - 1)
                    mm.then_inc(s_aused if j + 1 < chunks else s_acc, 1)
                n["acc"] += 1

            n["b"] = 1

            def ffn(experts, final=False):
                a0, b0, g0, lo0, ppv0 = n["a"], n["b"], n["g"], n["lo"], n["ppv"]
                if n["acc"]:
                    pe.wait_ge(s_accfree, n["acc"])
                for q in range(4):
                    nc.tensor.matmul(acc[:, q, :], zeros[:, 0:P], zeros[:, :], start=True, stop=False,
                                     skip_group_check=True)

                def gate_up(c, e, j):
                    slot = (a0 + c.rest) % 2
                    pe.wait_ge(s_alo, c.at(a0 + 1))
                    if c.rest == 0:
                        wait_pp()
                    else:
                        pe.wait_ge(s_ppv, c.half * 4 + (2 * c.rest + ppv0))
                    wh = hi_a[:, slot, :].rearrange("p (g k n) -> p g k n", g=2, k=KD)
                    wl = lo_a[:, slot, :].rearrange("p (g k n) -> p g k n", g=2, k=KD)
                    for tt in range(TT):
                        for k in range(KD):
                            ts = slice(tt * P, (tt + 1) * P)
                            mm = split3(pp[:, tt, :], uT_hi[:, k, ts], uT_lo[:, k, ts], wh[:, :, k, :],
                                        wl[:, :, k, :], k == 0, k == KD - 1)
                        mm.then_inc(s_pp, 1)

                def turn(c):
                    bank = (g0 + c.rest) % 2
                    pe.wait_ge(s_ppv, c.half * 4 + (2 * c.rest + 2 + ppv0))
                    pe.wait_ge(s_tlo, c.at(lo0 - 1))
                    for kk in range(2):
                        for tt in range(TT):
                            mm = nc.tensor.transpose(tp[:, bank, kk * S + tt * P:kk * S + (tt + 1) * P],
                                                     rows[:, tt, FCH + kk * P:FCH + (kk + 1) * P], ident[:, :])
                    mm.then_inc(s_tps, 1)

                def down(c, last):
                    pe.wait_ge(s_blo, c.at(b0 + 1))
                    pe.wait_ge(s_tlo, c.at(lo0 + 1))
                    for kk in range(2):
                        for tt in range(TT):
                            for h in range(2):
                                ts = slice(tt * P, (tt + 1) * P)
                                cs = slice(kk * 1024 + h * 512, kk * 1024 + (h + 1) * 512)
                                mm = split3(acc[:, tt * 2 + h, :], hT_hi[:, kk, ts], hT_lo[:, kk, ts],
                                            hi_b[:, cs], lo_b[:, cs], False, last and kk == 1)
                    mm.then_inc(s_acc if last else s_bused, 1)

                def head():
                    gate_up(Chunk(0, 0), 0, 0)
                    turn(Chunk(0, 0))

                def side_b(c, e, j):
                    down(c, False)
                    turn(c.next())

                def tail(c, e, j):
                    down(c, True)

                ffn_walk(pe, experts, gate_up, side_b, head, tail, final)
                k = experts * N_FCH
                n["a"] += k
                n["b"] += k
                n["g"] += k
                n["lo"] += k
                n["pp"] += 2 * k
                n["ppa"] += 2 * k
                n["ppv"] += 2 * k
                bank_free[0] = bank_free[1] = (s_tlo, n["lo"])
                n["acc"] += 1

            def attention(kind, q0, k0, v0, maps):
                items = maps // 2 if kind == "diff" else maps
                vw = 128 if kind == "diff" else HD
                m0, i0, tq0 = n["map"], n["item"], n["qkT"]

                def pair(p):
                    def cols(base, tt):
                        off = 0 if kind == "sw" and base == k0 else p * P
                        return rows[:, tt, base + off:base + off + P]
                    n["qkT"] += 1
                    group([(b * S + tt * P, cols(base, tt)) for b, base in enumerate((q0, k0)) for tt in range(TT)],
                          (s_qkT, n["qkT"]))

                def qk(m):
                    M = m0 + m
                    if M >= 2:
                        pe.wait_ge(s_sc, M - 1)
                    pe.wait_ge(s_qkT, tq0 + m // 2 + 1)
                    base = (m % 2) * HD
                    src = qkT[base:base + HD, (tq0 + m // 2) % 2, :]
                    for tt in range(TT):
                        mm = nc.tensor.matmul(acc[:, M % 2, tt * S:(tt + 1) * S], src[:, tt * P:(tt + 1) * P],
                                              src[:, S:2 * S], start=True, stop=True)
                    mm.then_inc(s_qk, 1)

                def pt(it):
                    I = i0 + it
                    if I >= 2:
                        pe.wait_ge(s_pte, I - 1)
                    if kind == "diff":
                        pe.wait_ge(s_comb, n["comb"] + it + 1)
                        w = bias[:, it % 2, :, :]
                    else:
                        pe.wait_ge(s_exp, m0 + it + 1)
                        w = sc[:, (m0 + it) % 2, :, :]
                    for kt in range(2):
                        for tt in range(TT):
                            mm = nc.tensor.transpose(acc[:, 2 + I % 2, kt * S + tt * P:kt * S + (tt + 1) * P],
                                                     w[:, tt, kt * P:(kt + 1) * P], ident[:, :])
                    mm.then_inc(s_pt, 1)

                def pv(it):
                    I = i0 + it
                    pe.wait_ge(s_pte, I + 1)
                    if I >= 2:
                        pe.wait_ge(s_o, I - 1)
                    if kind == "sw":
                        vc = v0 + (it % 2) * HD
                    else:
                        vc = v0 + it * vw
                    for tt in range(TT):
                        for kt in range(2):
                            mm = nc.tensor.matmul(pp[:, I % 2, tt * vw:(tt + 1) * vw],
                                                  pT[:, I % 2, kt, tt * P:(tt + 1) * P],
                                                  rows[:, kt, vc:vc + vw], start=(kt == 0), stop=(kt == 1))
                    mm.then_inc(s_pv, 1)

                per = maps // items
                wait_pp()
                if n["acc"]:
                    pe.wait_ge(s_accfree, n["acc"])
                if kind in ("sw", "diff"):
                    n["rows"] += 1
                    pe.wait_ge(s_rows, n["rows"])
                pair(0)
                for m in range(per):
                    qk(m)
                for it in range(items):
                    if per == 2 and it + 1 < items:
                        pair(it + 1)
                    if per == 1 and it % 2 == 0 and it + 2 < items:
                        pair(it // 2 + 1)
                    if it + 1 < items:
                        for m in range(per):
                            qk(per * (it + 1) + m)
                    pt(it)
                    if it >= 1:
                        pv(it - 1)
                pv(items - 1)
                n["map"] += maps
                n["item"] += items
                if kind == "diff":
                    n["comb"] += items
                pe.wait_ge(s_o, n["item"])

            def pooling():
                pe.wait_ge(s_pw, 32 + 16 * n["plc"])
                if n["acc"]:
                    pe.wait_ge(s_accfree, n["acc"])
                wait_pp()
                for g in range(4):
                    for st in range(TT):
                        mm = nc.tensor.matmul(acc[0:64, g // 2, (g % 2) * S:(g % 2 + 1) * S],
                                              rows[:, st, g * 64:(g + 1) * 64],
                                              merged[:, st, g * S:(g + 1) * S], start=(st == 0), stop=(st == 1))
                mm.then_inc(s_pla, 1)
                n["plc"] += 1
                pe.wait_ge(s_plb, n["plc"])
                for tt in range(TT):
                    for g in range(4):
                        mm = nc.tensor.matmul(acc[:, 2 + tt, g * 64:(g + 1) * 64],
                                              pT[0:64, g // 2, g % 2, tt * P:(tt + 1) * P], pool_w[:, g, :],
                                              start=True, stop=True)
                mm.then_inc(s_plc, 1)
                pe.wait_ge(s_plo, n["plc"])

            def router():
                wait_pp()
                pe.wait_ge(s_rlo, 1)
                for tt in range(TT):
                    for k in range(KD):
                        ts = slice(tt * P, (tt + 1) * P)
                        es = slice(k * N_EXPERTS, (k + 1) * N_EXPERTS)
                        mm = split3(pp[:, tt, 0:N_EXPERTS], uT_hi[:, k, ts], uT_lo[:, k, ts], rt_hi[:, es],
                                    rt_lo[:, es], k == 0, k == KD - 1)
                    mm.then_inc(s_pp, 1)
                n["pp"] += 2
                n["ppv"] += 2

            pe.wait_ge(s_const, 48)
            pe.wait_ge(s_zero, 3)
            pe.sem_inc(s_bused, 1)
            for i in range(N_LAYERS):
                transpose_rows(x, KD)
                wait_uT()
                for j in range(D_IN // 512):
                    project()
                pooling()
                attention("chunk", 256, 640, 1024, CHUNK_HEADS)
                attention("sb", 1408, 1792, 2176, SB_HEADS)
                transpose_rows(t, KD)
                wait_uT()
                project_out(KD, 512, uT_hi, uT_lo, 2)
                transpose_rows(x, KD)
                wait_uT()
                if i == 1:
                    router()
                ffn(N_EXPERTS if i == 1 else 1)
            for l in range(N_LAYERS):
                transpose_rows(t, KD)
                wait_uT()
                ffn(1)
                transpose_rows(t, KD)
                wait_uT()
                for kind, q0, k0, v0, maps, widths in (("na", 0, 512, 1024, 8, (512, 512, 512)),
                                                       ("sw", 1024, 512, 640, 8, (512, 256)),
                                                       ("diff", 0, 512, 1024, 8, (512, 512, 512))):
                    for width in widths:
                        project(width)
                    attention(kind, q0, k0, v0, maps)
                    for j in range(2):
                        project()
                    transpose_rows(rows, 4)
                    pe.wait_ge(s_tlo, n["lo"])
                    project_out(4, 1024, hT_hi, hT_lo, 1)
                transpose_rows(merged, KD)
                wait_uT()
                project_out(KD, 512, uT_hi, uT_lo, 2)
                transpose_rows(t, KD)
                wait_uT()
                ffn(1, l + 1 == N_LAYERS)

        @block.scalar
        def _(act):
            n = Tally()
            landed = [0, 0]
            used = []
            n["b"] = n["bu"] = 1

            def hi_chunk_a():
                slot = n["a"] % 2
                landed[slot] += 32
                act.wait_ge(s_al[slot], landed[slot])
                if n["a"] >= 2:
                    act.wait_ge(*used[n["a"] - 2])
                nc.scalar.activation(hi_a[:, slot, :], raw_a[:, slot, :], ACT.Copy).then_inc(s_ahi, 1)
                n["a"] += 1

            def hi_groups(dst, groups):
                for g in range(groups):
                    n["g"] += 1
                    act.wait_ge(s_tps, n["g"])
                    nc.scalar.activation(dst[:, 2 * g:2 * g + 2, :].rearrange("p k s -> p (k s)"),
                                         tp[:, (n["g"] - 1) % 2, :], ACT.Copy).then_inc(s_thi, 1)

            def project_copy(c0, width=512):
                hi_chunk_a()
                act.wait_ge(s_pp, n["pp"] + 1)
                nc.scalar.activation(rows[:, 0, c0:c0 + width], pp[:, 0, 0:width], ACT.Copy).then_inc(s_ppa, 2)
                n["pp"] += 2
                used.append((s_pp, n["pp"]))

            def out_chunks(chunks):
                for j in range(chunks):
                    hi_chunk_a()
                    if j + 1 < chunks:
                        n["aused"] += 1
                        used.append((s_aused, n["aused"]))
                    else:
                        used.append((s_acc, n["acc"] + 1))

            def ffn(experts, final=False):
                a1, b0, g0, pp0, bu0 = n["a"], n["b"], n["g"], n["pp"], n["bu"]
                last = experts * N_FCH - 1
                base = list(landed)

                def hi_next(c):
                    if final and isinstance(c.half, int) and c.at(0) == last:
                        return
                    slot = (a1 + c.rest) % 2
                    act.wait_ge(s_al[slot], c.turns(0) * 32 + (base[slot] + 32))
                    if c.rest == 0:
                        act.wait_ge(*used[-1])
                    else:
                        act.wait_ge(s_pp, c.half * 4 + (2 * c.rest + pp0))
                    nc.scalar.activation(hi_a[:, slot, :], raw_a[:, slot, :], ACT.Copy).then_inc(s_ahi, 1)

                def silu(c):
                    for tt in range(TT):
                        act.wait_ge(s_pp, c.half * 4 + (2 * c.rest + tt + 1 + pp0))
                        nc.scalar.activation(rows[:, tt, 0:FCH], pp[:, tt, 0:FCH], ACT.Silu).then_inc(s_ppa, 1)

                def down_side(c):
                    act.wait_ge(s_tps, c.at(g0 + 1))
                    nc.scalar.activation(hT_hi[:, 0:2, :].rearrange("p k s -> p (k s)"), tp[:, (g0 + c.rest) % 2, :],
                                         ACT.Copy).then_inc(s_thi, 1)
                    act.wait_ge(s_bl, c.half * 32 + 16 * (c.rest + b0))
                    act.wait_ge(s_bused, c.at(bu0))
                    nc.scalar.activation(hi_b[:, :], raw_b[:, :], ACT.Copy).then_inc(s_bhi, 1)

                def head():
                    hi_next(Chunk(0, 0))
                    silu(Chunk(0, 0))

                def body_a(c, e, j):
                    down_side(Chunk(c.half, c.rest - 1))
                    hi_next(c)
                    silu(c)

                ffn_walk(act, experts, body_a, lambda c, e, j: None, head, lambda c, e, j: down_side(c), final)
                k = experts * N_FCH
                for c in range(k):
                    landed[(a1 + c) % 2] += 32
                    used.append((s_pp, pp0 + 2 * (c + 1)))
                n["bu"] += k - 1
                n["a"] += k
                n["b"] += k
                n["g"] += k
                n["pp"] += 2 * k

            def squares(srcs, final=None):
                for k, (src, col, b) in enumerate(srcs):
                    w = 1
                    for d in src.shape[1:]:
                        w *= d
                    scratch = sc[:, :, :, :].rearrange("p s t k -> p (s t k)")[:, 0:w]
                    if len(src.shape) == 3:
                        scratch = scratch.rearrange("p (a b) -> p a b", a=src.shape[1])
                    if n["ss"]:
                        act.wait_ge(s_ss, n["ss"])
                    nc.scalar.activation(scratch, src, ACT.Square, bias=b, accum_out=ss[:, col:col + 1]) \
                      .then_inc(s_ss, 1)
                    n["ss"] += 1

            def soft_exp(m, kind):
                M = n["m0"] + m
                act.wait_ge(s_nm, M + 1)
                for tt in range(TT):
                    last = nc.scalar.activation(sc[:, M % 2, tt, :], sc[:, M % 2, tt, :], ACT.Exp,
                                                bias=negmax[:, M % 4, tt:tt + 1],
                                                accum_out=psums[:, M % 4, tt:tt + 1])
                if kind == "sw":
                    h = m // 2 + 4 * (m % 2)
                    last = nc.scalar.activation(esink[:, M % 4, :], negmax[:, M % 4, :], ACT.Exp,
                                                bias=sink[:, h:h + 1])
                last.then_inc(s_exp, 1)

            def sb_log(m):
                M = n["m0"] + m
                act.wait_ge(s_sc, M + 1)
                z, w = sc[:, M % 2, :, :], bias[:, m % 2, :, :]
                nc.scalar.activation(w, z, ACT.Abs).then_inc(s_ln, 1)
                act.wait_ge(s_ln, n["ln"] + 1)
                nc.scalar.activation(w, w, ACT.Exp, scale=-1.0).then_inc(s_ln, 1)
                act.wait_ge(s_ln, n["ln"] + 2)
                nc.scalar.activation(w, w, ACT.Ln, bias=1.0).then_inc(s_ln, 1)
                n["ln"] += 3

            def sb_exp(m):
                M = n["m0"] + m
                act.wait_ge(s_nm, M + 1)
                nc.scalar.activation(sc[:, M % 2, :, :], sc[:, M % 2, :, :], ACT.Exp).then_inc(s_exp, 1)

            def attention(kind, maps):
                items = maps // 2 if kind == "diff" else maps
                per = maps // items
                n["m0"], n["i0"] = n["map"], n["item"]

                def pair():
                    n["g"] += 1
                    act.wait_ge(s_tps, n["g"])
                    nc.scalar.activation(qkT[:, n["qkT"] % 2, :], tp[:, (n["g"] - 1) % 2, :], ACT.Copy) \
                      .then_inc(s_qkT, 1)
                    n["qkT"] += 1

                def soften(m):
                    if kind == "sb":
                        sb_log(m)
                        sb_exp(m)
                    else:
                        soft_exp(m, kind)

                def copy_pT(it):
                    I = n["i0"] + it
                    act.wait_ge(s_pt, I + 1)
                    if I >= 2:
                        act.wait_ge(s_pv, I - 1)
                    nc.scalar.activation(pT[:, I % 2, :, :].rearrange("p k s -> p (k s)"), acc[:, 2 + I % 2, :],
                                         ACT.Copy).then_inc(s_pte, 1)

                pair()
                for m in range(per):
                    soften(m)
                for it in range(items):
                    if per == 2 and it + 1 < items:
                        pair()
                    if per == 1 and it % 2 == 0 and it + 2 < items:
                        pair()
                    copy_pT(it)
                    if it + 1 < items:
                        for m in range(per):
                            soften(per * (it + 1) + m)
                n["map"] += maps
                n["item"] += items

            def wait_nmean():
                n["nmean"] += 1
                act.wait_ge(s_nmean, n["nmean"])

            act.wait_ge(s_zero, 3)
            act.wait_ge(s_const, 48)
            hi_chunk_a()
            act.wait_ge(s_rt, 16)
            nc.scalar.activation(rt_hi[:, :], rt[:, :], ACT.Copy).then_inc(s_rhi, 1)
            act.wait_ge(s_ext, 64)
            for i in range(N_LAYERS):
                hi_groups(uT_hi, 4)
                for j in range(D_IN // 512):
                    project_copy(512 * j)
                attention("chunk", CHUNK_HEADS)
                attention("sb", SB_HEADS)
                act.wait_ge(s_o, n["item"])
                squares([(t[:, tt, c0:c1], tt * 3 + k, 0.0) for tt in range(TT)
                         for k, (c0, c1) in enumerate(((0, 256), (256, 640), (640, 1024)))])
                hi_groups(uT_hi, 4)
                out_chunks(2)
                n["acc"] += 1
                wait_nmean()
                squares([(x[:, tt, :], tt, nmean[:, tt:tt + 1]) for tt in range(TT)])
                hi_groups(uT_hi, 4)
                if i == 1:
                    act.wait_ge(s_rnt, 1)
                    nc.scalar.activation(logit[:, :, :], logit[:, :, :], ACT.Exp).then_inc(s_rex, 1)
                    n["pp"] += 2
                ffn(N_EXPERTS if i == 1 else 1)
                n["acc"] += 1
                wait_nmean()
                squares([(x[:, tt, :], tt, nmean[:, tt:tt + 1]) for tt in range(TT)])
                n["x"] += 2
            for l in range(N_LAYERS):
                def pre():
                    act.wait_ge(s_x, n["x"])
                    squares([(x[:, tt, :], tt, 0.0) for tt in range(TT)])
                    hi_groups(uT_hi, 4)

                def post():
                    n["acc"] += 1
                    act.wait_ge(s_acc, n["acc"])
                    squares([(acc[:, 2 * tt:2 * tt + 2, :], tt, 0.0) for tt in range(TT)])
                    n["x"] += 1

                pre()
                ffn(1)
                post()
                act.wait_ge(s_lamv, l + 1)
                nc.scalar.activation(lam_e[:, :], lam_s[:, :], ACT.Exp).then_inc(s_lame, 1)
                pre()
                for br, (kind, cols) in enumerate((("na", ((0, 512), (512, 512), (1024, 512))),
                                                   ("sw", ((0, 512), (512, 256))),
                                                   ("diff", ((0, 512), (512, 512), (1024, 512))))):
                    for c0, width in cols:
                        project_copy(c0, width)
                    attention(kind, 8)
                    for j in range(2):
                        hi_chunk_a()
                        n["pp"] += 2
                        n["gl"] += 1
                        act.wait_ge(s_merge, n["gl"])
                        used.append((s_pp, n["pp"]))
                        g = rows[:, :, 1536 + 512 * j:2048 + 512 * j]
                        nc.scalar.activation(g, g, ACT.Sigmoid).then_inc(s_ppa, 2)
                    hi_groups(hT_hi, 2)
                    out_chunks(1)
                    n["acc"] += 1
                hi_groups(uT_hi, 4)
                out_chunks(2)
                post()
                pre()
                ffn(1, l + 1 == N_LAYERS)
                post()

        @block.vector
        def _(dve):
            n = Tally()

            def link(ins):
                n["dve"] += 1
                ins.then_inc(s_dve, 1)
                dve.wait_ge(s_dve, n["dve"])

            def signal(s):
                dve.sem_inc(s, 1)

            def lo_chunk_a():
                slot = n["a"] % 2
                n["a"] += 1
                dve.wait_ge(s_ahi, n["a"])
                nc.vector.tensor_tensor(lo_a[:, slot, :], raw_a[:, slot, :], hi_a[:, slot, :].bitcast(F32),
                                        ALU.subtract).then_inc(s_alo, 1)

            def lo_groups(hi, lo, groups):
                for g in range(groups):
                    n["g"] += 1
                    n["thi"] += 1
                    dve.wait_ge(s_thi, n["thi"])
                    nc.vector.tensor_tensor(lo[:, 2 * g:2 * g + 2, :].rearrange("p k s -> p (k s)"),
                                            tp[:, (n["g"] - 1) % 2, :],
                                            hi[:, 2 * g:2 * g + 2, :].rearrange("p k s -> p (k s)").bitcast(F32),
                                            ALU.subtract).then_inc(s_tlo, 1)

            def project_copy(c0, width=512):
                lo_chunk_a()
                n["pp"] += 2
                dve.wait_ge(s_pp, n["pp"])
                nc.vector.tensor_copy(rows[:, 1, c0:c0 + width], pp[:, 1, 0:width]).then_inc(s_ppv, 2)

            def gain():
                slot = n["vec"] % 2
                dve.wait_ge(s_vec[slot], 16 * (n["vec"] // 2 + 1))
                n["vec"] += 1
                return slot

            def wait_rstd():
                n["rstd"] += 1
                dve.wait_ge(s_rstd, n["rstd"])

            def ffn(experts, final=False):
                a1, b0, g0, hi0, ppa0 = n["a"], n["b"], n["g"], n["thi"], n["ppa"]

                def lo_next(c):
                    if final and isinstance(c.half, int) and c.at(0) == N_FCH - 1:
                        return
                    slot = (a1 + c.rest) % 2
                    dve.wait_ge(s_ahi, c.at(a1 + 1))
                    nc.vector.tensor_tensor(lo_a[:, slot, :], raw_a[:, slot, :], hi_a[:, slot, :].bitcast(F32),
                                            ALU.subtract).then_inc(s_alo, 1)

                def hidden(c, e):
                    for tt in range(TT):
                        dve.wait_ge(s_ppa, c.half * 4 + (2 * c.rest + tt + 1 + ppa0))
                        o, s, u = rows[:, tt, FCH:2 * FCH], rows[:, tt, 0:FCH], pp[:, tt, FCH:2 * FCH]
                        if experts == 1:
                            ins = nc.vector.tensor_tensor(o, s, u, ALU.mult)
                        else:
                            ins = nc.vector.scalar_tensor_tensor(out=o, in0=s, scalar=gates[:, tt, bass.ds(e, 1)],
                                                                 in1=u, op0=ALU.mult, op1=ALU.mult)
                        ins.then_inc(s_ppv, 1)

                def down_side(c):
                    dve.wait_ge(s_thi, c.at(hi0 + 1))
                    nc.vector.tensor_tensor(hT_lo[:, 0:2, :].rearrange("p k s -> p (k s)"), tp[:, (g0 + c.rest) % 2, :],
                                            hT_hi[:, 0:2, :].rearrange("p k s -> p (k s)").bitcast(F32),
                                            ALU.subtract).then_inc(s_tlo, 1)
                    dve.wait_ge(s_bhi, c.at(b0 + 1))
                    nc.vector.tensor_tensor(lo_b[:, :], raw_b[:, :], hi_b[:, :].bitcast(F32),
                                            ALU.subtract).then_inc(s_blo, 1)

                def head():
                    lo_next(Chunk(0, 0))
                    hidden(Chunk(0, 0), 0)

                def body_a(c, e, j):
                    down_side(Chunk(c.half, c.rest - 1))
                    lo_next(c)
                    hidden(c, e)

                ffn_walk(dve, experts, body_a, lambda c, e, j: None, head, lambda c, e, j: down_side(c), final)
                k = experts * N_FCH
                n["a"] += k
                n["b"] += k
                n["g"] += k
                n["thi"] += k
                n["pp"] += 2 * k
                n["ppa"] += 2 * k

            def layer_norm():
                n["acc"] += 1
                dve.wait_ge(s_acc, n["acc"])
                for tt in range(TT):
                    link(nc.vector.scalar_tensor_tensor(out=x[:, tt, :].rearrange("p (h c) -> p h c", h=2),
                                                        in0=x[:, tt, :].rearrange("p (h c) -> p h c", h=2),
                                                        scalar=ALPHA, in1=acc[:, 2 * tt:2 * tt + 2, :], op0=ALU.mult,
                                                        op1=ALU.add, accum_out=sm[:, tt:tt + 1]))
                signal(s_sum)
                signal(s_accfree)
                wait_rstd()
                g, b = gain(), gain()
                for tt in range(TT):
                    link(nc.vector.tensor_scalar(x[:, tt, :], x[:, tt, :], nmean[:, tt:tt + 1], rstd[:, tt:tt + 1],
                                                 ALU.add, ALU.mult))
                    link(nc.vector.tensor_tensor(x[:, tt, :], x[:, tt, :], vec[:, g, :], ALU.mult))
                    link(nc.vector.tensor_tensor(x[:, tt, :], x[:, tt, :], vec[:, b, :], ALU.add))
                signal(s_vecused)
                signal(s_vecused)
                signal(s_x)

            def rows_ready():
                signal(s_rows)

            def attention(kind, maps, dst, width):
                items = maps // 2 if kind == "diff" else maps
                per = maps // items
                m0, i0 = n["map"], n["item"]
                biased = kind in ("chunk", "na")

                def scores(m):
                    M = m0 + m
                    dve.wait_ge(s_qk, M + 1)
                    if kind != "diff":
                        if i0 + m >= 2:
                            dve.wait_ge(s_pt, i0 + m - 1)
                    s_in, s_o_ = acc[:, M % 2, :].rearrange("p (t k) -> p t k", t=TT), sc[:, M % 2, :, :]
                    if biased:
                        n["bias"] += 1
                        dve.wait_ge(s_bias, n["bias"])
                        add = bias[:, (n["bias"] - 1) % 2, :, ::-1]
                    else:
                        add = mask[:, :, :]
                    if kind == "diff":
                        ins = nc.vector.tensor_scalar(s_o_, s_in, SCALE, None, ALU.mult)
                    else:
                        ins = nc.vector.scalar_tensor_tensor(out=s_o_, in0=s_in, scalar=SCALE, in1=add, op0=ALU.mult,
                                                             op1=ALU.add)
                    link(ins)
                    signal(s_sc)
                    if biased:
                        signal(s_biasused)
                    if kind == "sb":
                        w = bias[:, m % 2, :, :]
                        n["ln"] += 3
                        dve.wait_ge(s_ln, n["ln"])
                        link(nc.vector.scalar_tensor_tensor(out=w, in0=s_o_, scalar=0.0, in1=w, op0=ALU.max,
                                                            op1=ALU.add))
                        for tt in range(TT):
                            link(nc.vector.tensor_tensor_scan(w[:, tt, ::-1], w[:, tt, ::-1],
                                                              zcol.to_broadcast([P, S]), 0.0, ALU.add, ALU.add))
                        nc.vector.tensor_tensor(s_o_, s_o_, w, ALU.subtract).then_inc(s_nm, 1)
                        return
                    if kind == "sw":
                        h = m // 2 + 4 * (m % 2)
                        link(nc.vector.tensor_reduce(negmax[:, M % 4, :], s_o_, AX_X, ALU.max, negate=True))
                        nc.vector.tensor_scalar(negmax[:, M % 4, :], negmax[:, M % 4, :], nsink[:, h:h + 1], None,
                                                ALU.min).then_inc(s_nm, 1)
                    else:
                        nc.vector.tensor_reduce(negmax[:, M % 4, :], s_o_, AX_X, ALU.max, negate=True) \
                          .then_inc(s_nm, 1)

                def combine(it):
                    M = m0 + 2 * it
                    dve.wait_ge(s_exp, M + 2)
                    if i0 + it >= 2:
                        dve.wait_ge(s_pt, i0 + it - 1)
                    for k in range(2):
                        link(nc.vector.reciprocal(rsum[:, (M + k) % 4, :], psums[:, (M + k) % 4, :]))
                    link(nc.vector.tensor_scalar(rsum[:, (M + 1) % 4, :], rsum[:, (M + 1) % 4, :], nlam, None,
                                                 ALU.mult))
                    for tt in range(TT):
                        w = bias[:, it % 2, tt, :]
                        link(nc.vector.tensor_scalar(w, sc[:, M % 2, tt, :], rsum[:, M % 4, tt:tt + 1], None,
                                                     ALU.mult))
                        link(nc.vector.scalar_tensor_tensor(out=w, in0=sc[:, (M + 1) % 2, tt, :],
                                                            scalar=rsum[:, (M + 1) % 4, tt:tt + 1], in1=w,
                                                            op0=ALU.mult, op1=ALU.add))
                    signal(s_comb)

                def output(it):
                    I, M = i0 + it, m0 + it
                    dve.wait_ge(s_pv, I + 1)
                    vw = 128 if kind == "diff" else HD
                    if kind == "sw":
                        h = it // 2 + 4 * (it % 2)
                    else:
                        h = it
                    src = pp[:, I % 2, 0:2 * vw].rearrange("p (t d) -> p t d", t=TT)
                    o = dst[:, :, h * vw:(h + 1) * vw]
                    if kind in ("sb", "diff"):
                        ins = nc.vector.tensor_copy(o, src)
                    else:
                        if kind == "sw":
                            link(nc.vector.tensor_tensor(psums[:, M % 4, :], psums[:, M % 4, :], esink[:, M % 4, :],
                                                         ALU.add))
                        link(nc.vector.reciprocal(rsum[:, M % 4, :], psums[:, M % 4, :]))
                        ins = nc.vector.tensor_tensor(o, src, rsum[:, M % 4, :].unsqueeze(2).to_broadcast([P, TT, vw]),
                                                      ALU.mult)
                    ins.then_inc(s_o, 1)

                if not biased and kind != "diff":
                    n["maskl"] += 1
                    dve.wait_ge(s_mask, 16 * mask_index[kind][n["layer"]])
                for m in range(per):
                    scores(m)
                if kind == "diff":
                    combine(0)
                for it in range(items):
                    if it + 1 < items:
                        for m in range(per):
                            scores(per * (it + 1) + m)
                        if kind == "diff":
                            combine(it + 1)
                    if it >= 1:
                        output(it - 1)
                output(items - 1)
                n["map"] += maps
                n["item"] += items
                dve.wait_ge(s_o, n["item"])
                if kind in ("sb", "sw"):
                    signal(s_maskused)

            mask_index = {"sb": (2, 4), "sw": (6, 8)}

            def rotate(width, regroup):
                heads = width // HD
                for tt in range(TT):
                    v = rows[:, tt, 0:width].rearrange("p (h d) -> p h d", d=HD)
                    w = t[:, tt, 0:width].rearrange("p (h d) -> p h d", d=HD)
                    for half in range(2):
                        o = slice(32 * half, 32 * half + 32)
                        i_ = slice(32 - 32 * half, 64 - 32 * half)
                        ins = nc.vector.tensor_tensor(w[:, :, o], v[:, :, i_],
                                                      rope[:, 1, tt, o].unsqueeze(1).to_broadcast([P, heads, 32]),
                                                      ALU.mult)
                        if half:
                            link(ins)
                    link(nc.vector.tensor_tensor(v, v, rope[:, 0, tt, :].unsqueeze(1).to_broadcast([P, heads, HD]),
                                                 ALU.mult))
                    if not regroup:
                        link(nc.vector.tensor_tensor(v, v, w, ALU.add))
                        continue
                    link(nc.vector.tensor_tensor(v[:, 8:heads, :], v[:, 8:heads, :], w[:, 8:heads, :], ALU.add))
                    link(nc.vector.tensor_tensor(
                        rows[:, tt, 1024:1536].rearrange("p (q a d) -> p a q d", a=2, d=HD),
                        v[:, 0:8, :].rearrange("p (a q) d -> p a q d", a=2),
                        w[:, 0:8, :].rearrange("p (a q) d -> p a q d", a=2), ALU.add))

            nc.vector.memset(zeros[:, :], 0.0).then_inc(s_zero, 1)
            nc.vector.memset(stat[:, :], 0.0).then_inc(s_zero, 1)
            dve.wait_ge(s_zero, 2)
            nc.vector.memset(half_pow, -0.5).then_inc(s_zero, 1)
            dve.wait_ge(s_zero, 3)
            dve.wait_ge(s_const, 48)
            dve.wait_ge(s_xin, 16)
            signal(s_rows)
            signal(s_blo)
            dve.wait_ge(s_ext, 64)
            lo_chunk_a()
            dve.wait_ge(s_rhi, 1)
            nc.vector.tensor_tensor(rt_lo[:, :], rt[:, :], rt_hi[:, :].bitcast(F32), ALU.subtract).then_inc(s_rlo, 1)

            for i in range(N_LAYERS):
                n["layer"] = i
                lo_groups(uT_hi, uT_lo, 4)
                for j in range(D_IN // 512):
                    project_copy(512 * j)
                n["ppa"] += 10
                dve.wait_ge(s_pla, i + 1)
                nc.vector.tensor_copy(pT[0:64, :, :, :].rearrange("p a b s -> p (a b s)"),
                                      acc[0:64, 0:2, :].rearrange("p a s -> p (a s)")).then_inc(s_plb, 1)
                slot = gain()
                dve.wait_ge(s_plc, i + 1)
                for tt in range(TT):
                    link(nc.vector.tensor_tensor(t[:, tt, 0:D_POOL], acc[:, 2 + tt, 0:D_POOL], vec[:, slot, 0:D_POOL],
                                                 ALU.mult))
                signal(s_vecused)
                signal(s_plo)
                n["g"] += 3
                attention("chunk", CHUNK_HEADS, t[:, :, 256:640], 384)
                n["g"] += 3
                attention("sb", SB_HEADS, t[:, :, 640:1024], 384)
                wait_rstd()
                slot = gain()
                for tt in range(TT):
                    for k, (c0, c1) in enumerate(((0, 256), (256, 640), (640, 1024))):
                        link(nc.vector.scalar_tensor_tensor(out=t[:, tt, c0:c1], in0=t[:, tt, c0:c1],
                                                            scalar=rstd[:, tt * 3 + k:tt * 3 + k + 1],
                                                            in1=vec[:, slot, c0:c1], op0=ALU.mult, op1=ALU.mult))
                signal(s_vecused)
                rows_ready()
                lo_groups(uT_hi, uT_lo, 4)
                lo_chunk_a()
                lo_chunk_a()
                layer_norm()
                rows_ready()
                lo_groups(uT_hi, uT_lo, 4)
                if i == 1:
                    n["pp"] += 2
                    dve.wait_ge(s_pp, n["pp"])
                    for tt in range(TT):
                        link(nc.vector.tensor_copy(logit[:, tt, :], pp[:, tt, 0:8]))
                    for tt in range(TT):
                        lj = logit[:, tt, :].unsqueeze(1).to_broadcast([P, 8, 8])
                        le = logit[:, tt, :].unsqueeze(2).to_broadcast([P, 8, 8])
                        c1v = cmp1[:, :].rearrange("p (e j) -> p e j", e=8)
                        c2v = cmp2[:, :].rearrange("p (e j) -> p e j", e=8)
                        link(nc.vector.tensor_tensor(c1v, lj, le, ALU.is_gt))
                        link(nc.vector.tensor_tensor(c2v, lj, le, ALU.is_equal))
                        link(nc.vector.tensor_tensor(cmp2[:, :], cmp2[:, :], earlier[:, :], ALU.mult))
                        link(nc.vector.tensor_tensor(cmp1[:, :], cmp1[:, :], cmp2[:, :], ALU.add))
                        link(nc.vector.tensor_reduce(rank, c1v, AX_X, ALU.add))
                        link(nc.vector.tensor_scalar(gates[:, tt, :], rank, 2.0, None, ALU.is_lt))
                        link(nc.vector.tensor_reduce(top[:, tt:tt + 1], logit[:, tt, :], AX_X, ALU.max))
                        link(nc.vector.tensor_scalar(logit[:, tt, :], logit[:, tt, :], top[:, tt:tt + 1], None,
                                                     ALU.subtract))
                    signal(s_rnt)
                    dve.wait_ge(s_rex, 1)
                    for tt in range(TT):
                        link(nc.vector.tensor_tensor(gates[:, tt, :], gates[:, tt, :], logit[:, tt, :], ALU.mult))
                        link(nc.vector.tensor_reduce(gsum[:, tt:tt + 1], gates[:, tt, :], AX_X, ALU.add))
                        link(nc.vector.reciprocal(gsum[:, tt:tt + 1], gsum[:, tt:tt + 1]))
                        link(nc.vector.tensor_scalar(gates[:, tt, :], gates[:, tt, :], gsum[:, tt:tt + 1], None,
                                                     ALU.mult))
                    signal(s_ppv)
                    signal(s_ppv)
                ffn(N_EXPERTS if i == 1 else 1)
                layer_norm()
                if i + 1 < N_LAYERS:
                    rows_ready()

            for l in range(N_LAYERS):
                n["layer"] = l

                def pre():
                    wait_rstd()
                    slot = gain()
                    for tt in range(TT):
                        link(nc.vector.scalar_tensor_tensor(out=t[:, tt, :], in0=x[:, tt, :], scalar=rstd[:, tt:tt + 1],
                                                            in1=vec[:, slot, :], op0=ALU.mult, op1=ALU.mult))
                    signal(s_vecused)
                    rows_ready()
                    lo_groups(uT_hi, uT_lo, 4)

                def post():
                    n["acc"] += 1
                    wait_rstd()
                    slot = gain()
                    for tt in range(TT):
                        o = t[:, tt, :]
                        link(nc.vector.scalar_tensor_tensor(out=o.rearrange("p (h c) -> p h c", h=2),
                                                            in0=acc[:, 2 * tt:2 * tt + 2, :],
                                                            scalar=rstd[:, tt:tt + 1],
                                                            in1=vec[:, slot, :].rearrange("p (h c) -> p h c", h=2),
                                                            op0=ALU.mult, op1=ALU.mult))
                        link(nc.vector.tensor_tensor(x[:, tt, :], x[:, tt, :], o, ALU.add))
                    signal(s_vecused)
                    signal(s_accfree)
                    signal(s_x)

                pre()
                ffn(1)
                post()
                dve.wait_ge(s_lam, 80 * (l + 1))
                for k in range(2):
                    link(nc.vector.tensor_tensor(lam4[:, 2 * k, :], lam4[:, 2 * k, :], lam4[:, 2 * k + 1, :],
                                                 ALU.mult))
                    link(nc.vector.tensor_reduce(lam_s[:, k:k + 1], lam4[:, 2 * k, :], AX_X, ALU.add))
                link(nc.vector.tensor_scalar(nsink, sink[:, :], -1.0, None, ALU.mult))
                signal(s_lamv)
                dve.wait_ge(s_lame, l + 1)
                lam_init = 0.8 - 0.6 * math.exp(-0.3 * l)
                link(nc.vector.tensor_tensor(nlam, lam_e[:, 1:2], lam_e[:, 0:1], ALU.subtract))
                link(nc.vector.tensor_scalar(nlam, nlam, -lam_init, None, ALU.add))
                pre()
                for br, (kind, cols) in enumerate((("na", ((0, 512), (512, 512), (1024, 512))),
                                                   ("sw", ((0, 512), (512, 256))),
                                                   ("diff", ((0, 512), (512, 512), (1024, 512))))):
                    for c0, width in cols:
                        project_copy(c0, width)
                        n["ppa"] += 2
                    if kind != "na":
                        dve.wait_ge(s_ppa, n["ppa"])
                        rotate(640 if kind == "sw" else 1024, kind == "sw")
                        rows_ready()
                    n["g"] += 4
                    attention(kind, 8, rows[:, :, 0:512], 512)
                    if kind == "diff":
                        o = rows[:, :, 0:512]
                        link(nc.vector.tensor_tensor(t[:, :, 0:512], o, o, ALU.mult))
                        link(nc.vector.tensor_reduce(ss[:, :].rearrange("p (t h) -> p t h", t=TT),
                                                     t[:, :, 0:512].rearrange("p t (h d) -> p t h d", h=4),
                                                     AX_X, ALU.add))
                        signal(s_sum)
                        wait_rstd()
                        slot = gain()
                        for tt in range(TT):
                            v = rows[:, tt, 0:512].rearrange("p (h d) -> p h d", h=4)
                            link(nc.vector.tensor_tensor(v, v, rstd[:, 4 * tt:4 * tt + 4].unsqueeze(2)
                                                         .to_broadcast([P, 4, 128]), ALU.mult))
                            link(nc.vector.tensor_tensor(v, v, vec[:, slot, 0:128].unsqueeze(1)
                                                         .to_broadcast([P, 4, 128]), ALU.mult))
                        signal(s_vecused)
                    rows_ready()
                    slot = gain()
                    for j in range(2):
                        lo_chunk_a()
                        for tt in range(TT):
                            n["pp"] += 1
                            dve.wait_ge(s_pp, n["pp"])
                            ins = nc.vector.tensor_tensor(rows[:, tt, 1536 + 512 * j:2048 + 512 * j], pp[:, tt, :],
                                                          vec[:, slot, 512 * j:512 * (j + 1)], ALU.add)
                            if tt == 1:
                                link(ins)
                        signal(s_merge)
                        signal(s_ppv)
                        signal(s_ppv)
                        n["ppa"] += 2
                    signal(s_vecused)
                    lo_groups(hT_hi, hT_lo, 2)
                    lo_chunk_a()
                    n["acc"] += 1
                    dve.wait_ge(s_acc, n["acc"])
                    dve.wait_ge(s_ppa, n["ppa"])
                    for tt in range(TT):
                        gate = rows[:, tt, 1536:2560].rearrange("p (h c) -> p h c", h=2)
                        o = (merged if br == 0 else t)[:, tt, :].rearrange("p (h c) -> p h c", h=2)
                        link(nc.vector.tensor_tensor(o, gate, acc[:, 2 * tt:2 * tt + 2, :], ALU.mult))
                        if br:
                            link(nc.vector.tensor_tensor(merged[:, tt, :], merged[:, tt, :], t[:, tt, :], ALU.add))
                    signal(s_accfree)
                rows_ready()
                lo_groups(uT_hi, uT_lo, 4)
                lo_chunk_a()
                lo_chunk_a()
                post()
                pre()
                ffn(1, l + 1 == N_LAYERS)
                post()

        @block.gpsimd
        def _(g):
            n = Tally()

            def link(ins):
                n["pool"] += 1
                ins.then_inc(s_pool, 1)
                g.wait_ge(s_pool, n["pool"])

            def load_gain():
                k = n["vec"]
                if k < len(GAINS):
                    if k >= 2:
                        g.wait_ge(s_vecused, k - 1)
                    src = GAINS[k]
                    w = src.shape[0]
                    g.dma_start(vec[:, k % 2, 0:w], row_bcast(src)).then_inc(s_vec[k % 2], 16)
                    n["vec"] += 1

            def deviations(parts, factor=1.0):
                for c0, c1, width, eps in parts:
                    link(nc.gpsimd.tensor_scalar(ss[:, c0:c1], ss[:, c0:c1], 1.0 / (width * factor ** 2),
                                                 eps / factor ** 2, ALU.mult, ALU.add))
                c1 = parts[-1][1]
                nc.gpsimd.tensor_tensor(rstd[:, 0:c1], ss[:, 0:c1], half_pow[:, 0:c1], ALU.pow).then_inc(s_rstd, 1)

            def rms(count, parts, factor=1.0):
                n["ss"] += count
                g.wait_ge(s_ss, n["ss"])
                deviations(parts, factor)

            def load_mask(which):
                if n["maskused"]:
                    g.wait_ge(s_maskused, n["maskused"])
                g.dma_start(mask[:, :, :], a["c_masks"][which].rearrange("(t p) k -> p t k", p=P)).then_inc(s_mask, 16)
                n["mask"] += 1

            def biases(load, heads, per_load):
                g.wait_ge(s_mask, 16 * n["mask"])

                def start(h):
                    if n["bl"] >= 2:
                        g.wait_ge(s_biasused, n["bl"] - 1)
                    load(h, n["bl"] % 2)
                    n["bl"] += 1

                start(0)
                for h in range(heads):
                    if h + 1 < heads:
                        start(h + 1)
                    k = n["bias"]
                    n["landed%d" % (k % 2)] += per_load
                    g.wait_ge(s_biasl[k % 2], n["landed%d" % (k % 2)])
                    nc.gpsimd.tensor_tensor(bias[:, k % 2, :, :], bias[:, k % 2, :, :], mask[:, :, :], ALU.add) \
                      .then_inc(s_bias, 1)
                    n["bias"] += 1

            def layer_norm():
                n["sum"] += 1
                g.wait_ge(s_sum, n["sum"])
                nc.gpsimd.tensor_scalar(nmean, sm, -1.0 / D, None, ALU.mult).then_inc(s_nmean, 1)
                rms(2, [(0, 2, D, LN_EPS)])
                load_gain()
                load_gain()

            g.dma_start(ident[:, :], a["c_ident"]).then_inc(s_const, 16)
            g.dma_start(rope[:, :, :, :], a["c_rope"].rearrange("c (t p) d -> p c t d", p=P)).then_inc(s_const, 16)
            g.dma_start(earlier[:, :], a["c_earlier"]).then_inc(s_const, 16)
            g.dma_start(rt[:, :].rearrange("p (k e) -> p k e", k=KD),
                        a["moe_router"][0].rearrange("(k p) e -> p k e", p=P)).then_inc(s_rt, 16)
            g.dma_start(rows[0:12, 0, 127:384], a["rel_bias"].rearrange("l h r -> (l h) r")).then_inc(s_ext, 16)
            g.dma_start(rows[0:112, 1, 48:79], a["rpb_rows"]).then_inc(s_ext, 16)
            load_gain()
            load_gain()
            g.wait_ge(s_ext, 32)
            nc.gpsimd.tensor_copy(rows[0:12, 0, 0:127], rows[0:12, 0, 127:128].to_broadcast([12, 127]))
            nc.gpsimd.tensor_copy(rows[0:12, 0, 384:511], rows[0:12, 0, 383:384].to_broadcast([12, 127]))
            nc.gpsimd.tensor_copy(rows[0:112, 1, 0:48], rows[0:112, 1, 48:49].to_broadcast([112, 48]))
            link(nc.gpsimd.tensor_copy(rows[0:112, 1, 79:127], rows[0:112, 1, 78:79].to_broadcast([112, 48])))
            g.dma_start(ext1, rows[0:12, 0, 0:511]).then_inc(s_ext, 16)
            g.dma_start(ext2, rows[0:112, 1, 0:127]).then_inc(s_ext, 16)
            g.wait_ge(s_ext, 64)
            g.wait_ge(s_zero, 3)
            g.dma_start(merged[:, :, :].rearrange("p s (g t) -> p s g t", g=4),
                        a["c_pool"].rearrange("(s p) g t -> p s g t", p=P)).then_inc(s_pw, 16)

            for i in range(N_LAYERS):
                g.dma_start(pool_w[:, :, :], a["pool_w"][i].rearrange("g c d -> c g d")).then_inc(s_pw, 16)
                load_mask(0)

                def chunk_bias(h, slot):
                    src = bass.AP(ext1.tensor, (i * CHUNK_HEADS + h) * 511, [[1, P], [P, TT], [1, S]])
                    g.dma_start(bias[:, slot, :, :], src).then_inc(s_biasl[slot], 16)

                biases(chunk_bias, CHUNK_HEADS, 16)
                load_gain()
                g.wait_ge(s_bias, n["bias"])
                load_mask(1)
                n["maskused"] += 1
                rms(6, [(3 * tt + k, 3 * tt + k + 1, w, RMS_EPS) for tt in range(TT)
                        for k, w in enumerate((D_POOL, D_CHUNK, D_SB))])
                load_gain()
                layer_norm()
                layer_norm()
            for l in range(N_LAYERS):
                rms(2, [(0, 2, D, RMS_EPS)])
                load_gain()
                for k, name in enumerate(("q1", "k1", "q2", "k2")):
                    g.dma_start(lam4[:, k, :], row_bcast(a["diff_lambda_%s_2" % name][l])).then_inc(s_lam, 16)
                g.dma_start(sink[:, :], row_bcast(a["sw_sink_2"][l])).then_inc(s_lam, 16)
                rms(2, [(0, 2, D, RMS_EPS)], 0.5)
                load_gain()
                rms(2, [(0, 2, D, RMS_EPS)])
                load_gain()
                load_mask(2)

                def na_bias(h, slot):
                    for r in range(NA_ROWS):
                        src = bass.AP(ext2.tensor, ((l * NA_HEADS + h) * 7 + r) * 127,
                                      [[1, GRID_W], [127, NA_ROWS], [1, GRID_W]])
                        dst = bias[64 * (r % 2):64 * (r % 2) + 64, slot, r // 2, :]
                        g.dma_start(dst.rearrange("p (a b) -> p a b", a=NA_ROWS), src).then_inc(s_biasl[slot], 16)

                biases(na_bias, NA_HEADS, 64)
                g.wait_ge(s_bias, n["bias"])
                load_mask(3)
                n["maskused"] += 1
                load_gain()
                load_gain()
                n["sum"] += 1
                g.wait_ge(s_sum, n["sum"])
                lam_init = 0.8 - 0.6 * math.exp(-0.3 * l)
                deviations([(0, 8, 128, RMS_EPS)], 1.0 - lam_init)
                load_gain()
                load_gain()
                rms(2, [(0, 2, D, RMS_EPS)])
                load_gain()
                rms(2, [(0, 2, D, RMS_EPS)])
                load_gain()
                rms(2, [(0, 2, D, RMS_EPS)], 0.5)
                load_gain()


NAMES = ["x", "w_in", "pool_w", "pool_scale", "rel_bias", "g_mix", "w_out", "ln1_g", "ln1_b", "ln2_g", "ln2_b",
         "ffn_wg", "ffn_wu", "ffn_wd", "moe_router", "moe_wg", "moe_wu", "moe_wd", "ffn1_pre_g_2", "ffn1_w_gu_2",
         "ffn1_w_down_2", "ffn1_post_g_2", "mix_pre_g_2", "w_in_2", "sw_sink_2", "diff_lambda_q1_2",
         "diff_lambda_k1_2", "diff_lambda_q2_2", "diff_lambda_k2_2", "diff_subln_g_2", "w_branch_2", "b_gate_2",
         "w_out_2", "mix_post_g_2", "ffn2_pre_g_2", "ffn2_w_gu_2", "ffn2_w_down_2", "ffn2_post_g_2"]


def kernel(**inputs):
    import concourse.bacc as bacc
    from concourse.bass_utils import run_bass_kernel_spmd as run

    nc = bacc.Bacc("TRN2", target_bir_lowering=False, num_devices=1, dynamic_dma_scratch_size=2048)
    arrays = {name: np.ascontiguousarray(inputs[name]) for name in NAMES}
    arrays["rpb_rows"] = np.ascontiguousarray(np.asarray(inputs["na_rpb_2"])[:, :, 4:11, :][:, :, ::-1, ::-1]
                                              .reshape(N_LAYERS * NA_HEADS * 7, 31))
    arrays.update(shape_constants())
    aps = {}
    for name, v in arrays.items():
        aps[name] = nc.dram_tensor("in_" + name, v.shape, mybir.dt.from_np(v.dtype), kind="ExternalInput").ap()
    out = nc.dram_tensor("out_0", (1, S, D), F32, kind="ExternalOutput").ap()
    program(nc, aps, out)
    r = run(nc, [{"in_" + name: v for name, v in arrays.items()}], core_ids=[0])
    return r.results[0]["out_0"]
```

```python
import math
from contextlib import ExitStack

import numpy as np

import concourse.bass as bass
from concourse import mybir

F32 = mybir.dt.float32
F32R = mybir.dt.float32r
I32 = mybir.dt.int32
BF16 = mybir.dt.bfloat16
ALU = mybir.AluOpType
ACT = mybir.ActivationFunctionType
AX_X = mybir.AxisListType.X

P = 128
D = 1024
S = 256
TT = S // P
KD = D // P
HD = 64
N_LAYERS = 2
FF = 2816
FCH = 256
N_FCH = FF // FCH
N_EXPERTS = 8
CHUNK_HEADS = 6
SB_HEADS = 6
NA_HEADS = 8
SW_HEADS = 8
DIFF_HEADS = 4
D_POOL = 256
D_CHUNK = 384
D_SB = 384
D_IN = 2560
REL_CLIP = 128
NA_ROWS = 4
GRID_W = 64
ALPHA = (2.0 * N_LAYERS) ** 0.25
LN_EPS = 1e-5
RMS_EPS = 1e-6
NEG = -1e30
SCALE = 1.0 / math.sqrt(HD)
POOL_WINDOWS = (2, 4, 8, 16)

QA, KA, VA, QB, KB, QC, KC, VC, GL = 0, 512, 1024, 1536, 2048, 2304, 2816, 3328, 3840


def shape_constants():
    q = np.arange(S)[:, None]
    k = np.arange(S)[None, :]
    chunk_mask = np.where(k // 64 <= q // 64, 0.0, NEG)[:, ::-1]
    sb_mask = np.where(k < q, 0.0, NEG)
    sw_mask = np.where(np.abs(q - k) <= 128, 0.0, NEG)
    c0 = np.clip(q % GRID_W - 8, 0, GRID_W - 16)
    na_mask = np.where((k % GRID_W >= c0) & (k % GRID_W < c0 + 16), 0.0, NEG)[:, ::-1]
    masks = np.stack([chunk_mask, sb_mask, na_mask, sw_mask]).astype(np.float32)
    pos = np.arange(S, dtype=np.float32)
    inv = np.float32(10000.0) ** (-np.arange(0, HD, 2, dtype=np.float32) / np.float32(HD))
    ang = (pos[:, None] * inv[None, :]).astype(np.float32)
    ang = np.concatenate([ang, ang], axis=1)
    sign = np.concatenate([-np.ones(32), np.ones(32)])[None, :]
    rope = np.stack([np.cos(ang), np.sin(ang) * sign]).astype(np.float32)
    pool = np.zeros((S, 4, S), np.float64)
    for g, w in enumerate(POOL_WINDOWS):
        for t in range(S):
            lo = max(0, t - w + 1)
            pool[lo:t + 1, g, t] += 1.0 / min(t + 1, w)
            pool[t, g, t] -= 1.0
    slots = np.concatenate([np.broadcast_to(np.arange(P), (P, P)), np.triu(np.ones((P, P)), 1), np.ones((P, P))], axis=1)
    earlier = np.broadcast_to(np.tril(np.ones((8, 8)), -1).reshape(1, 64), (P, 64))
    return {"c_slots": slots.astype(np.float32), "c_masks": masks, "c_rope": rope, "c_pool": pool.astype(np.float32),
            "c_ident": np.eye(P, dtype=np.float32), "c_earlier": np.ascontiguousarray(earlier, dtype=np.float32)}


class Chunk:

    def __init__(self, half, rest):
        self.half, self.rest = half, rest

    def at(self, base):
        return self.half * 2 + (self.rest + base)

    def turns(self, first):
        return self.half + (self.rest // 2 + first)

    def next(self, n=1):
        return Chunk(self.half, self.rest + n)


class Expert:

    def __init__(self, index, odd):
        self.index, self.odd = index, odd


class Tally(dict):

    def __missing__(self, key):
        return 0


def program(nc, a, out):
    with ExitStack() as ctx:
        def sb(name, shape, dt=F32):
            return ctx.enter_context(nc.sbuf_tensor(name, shape, dt))

        def sem(name):
            return ctx.enter_context(nc.semaphore(name))

        with nc.sbuf_tensor("x_hi", [P, TT, D], F32R) as x_hi, \
                nc.sbuf_tensor("kept", [P, 2 * FCH], F32) as _, \
                nc.sbuf_tensor("x_lo", [P, TT, D], F32R) as x_lo, \
                nc.sbuf_tensor("y_hi", [P, D], F32R) as y_hi, \
                nc.sbuf_tensor("y_lo", [P, D], F32R) as y_lo:
            pass
        t = sb("t", [P, TT, D])
        rows = sb("rows", [P, TT, D_IN])
        raw_a = sb("raw_a", [P, 2, 4096])
        hi_a = sb("hi_a", [P, 2, 4096], F32R)
        lo_a = sb("lo_a", [P, 2, 4096], F32R)
        raw_b = sb("raw_b", [P, 2048])
        hi_b = sb("hi_b", [P, 2048], F32R)
        lo_b = sb("lo_b", [P, 2048], F32R)
        x = sb("x", [P, TT, D])
        uT_hi = sb("uT_hi", [P, KD, S], F32R)
        uT_lo = sb("uT_lo", [P, KD, S], F32R)
        hT_hi = sb("hT_hi", [P, 4, S], F32R)
        hT_lo = sb("hT_lo", [P, 4, S], F32R)
        merged = sb("merged", [P, TT, D])
        vec = sb("vec", [P, 2, D])
        qkT = sb("qkT", [P, 2, 512])
        sc = sb("sc", [P, 2, TT, S])
        pT = sb("pT", [P, 2, TT, S])
        bias = sb("bias", [P, 2, TT, S])
        mask = sb("mask", [P, TT, S])
        ident = sb("ident", [P, P])
        rope = sb("rope", [P, 2, TT, HD])
        zeros = sb("zeros", [P, 512], BF16)
        stat = sb("stat", [P, 256])
        earlier = sb("earlier", [P, 64])
        rt = sb("rt", [P, 64])
        rt_hi = sb("rt_hi", [P, 64], F32R)
        rt_lo = sb("rt_lo", [P, 64], F32R)
        cmp1 = sb("cmp1", [P, 64])
        cmp2 = sb("cmp2", [P, 64])
        lam4 = sb("lam4", [P, 4, 64])
        pool_w = lam4[0:64, :, :]
        sink = sb("sink", [P, 8])

        ss = stat[:, 0:8]
        rstd = stat[:, 8:16]
        sm = stat[:, 16:18]
        nmean = stat[:, 18:20]
        half_pow = stat[:, 20:28]
        negmax = stat[:, 32:40].rearrange("p (s t) -> p s t", t=TT)
        psums = stat[:, 40:48].rearrange("p (s t) -> p s t", t=TT)
        esink = stat[:, 48:56].rearrange("p (s t) -> p s t", t=TT)
        rsum = stat[:, 56:64].rearrange("p (s t) -> p s t", t=TT)
        logit = stat[:, 64:80].rearrange("p (t e) -> p t e", t=TT)
        top = stat[:, 80:82]
        rank = stat[:, 96:104]
        gates = stat[:, 104:120].rearrange("p (t e) -> p t e", t=TT)
        gsum = stat[:, 120:122]
        lam_s = stat[:, 124:126]
        lam_e = stat[:, 126:128]
        nlam = stat[:, 128:129]
        nsink = stat[:, 136:144]
        zcol = stat[:, 144:145]
        chosen = stat[:, 160:176].rearrange("p (t e) -> p t e", t=TT)
        slot_of = stat[:, 176:192].rearrange("p (t e) -> p t e", t=TT)
        most = stat[:, 192:193]
        crowded = sb("crowded", [P, 1], I32)

        slot_ids = bias[:, 0, 0, 0:P]
        before_op = bias[:, 0, 0, P:2 * P]
        any_op = bias[:, 0, 1, 0:P]

        def pick(odd):
            return (hT_hi, hT_lo)[odd][:, 2, :]

        def put(odd):
            return (hT_hi, hT_lo)[odd][:, 3, :]


        acc = ctx.enter_context(nc.psum_tensor("acc", [P, 4, 512], F32))
        pp = ctx.enter_context(nc.psum_tensor("pp", [P, TT, 512], F32))
        tp = ctx.enter_context(nc.psum_tensor("tp", [P, 2, 512], F32))

        ext1 = nc.dram_tensor("chunk_bias_rows", [12, 511], F32, kind="Internal").ap()
        na_bias = nc.dram_tensor("na_bias", [NA_HEADS, S, S], F32, kind="Internal").ap()
        ext2 = nc.dram_tensor("na_bias_rows", [112, 127], F32, kind="Internal").ap()

        s_const = sem("s_const")
        s_zero = sem("s_zero")
        s_xin = sem("s_xin")
        s_al = [sem("s_al0"), sem("s_al1")]
        s_bl = sem("s_bl")
        s_ahi = sem("s_ahi")
        s_ahalf = sem("s_ahalf")
        s_alo = sem("s_alo")
        s_aused = sem("s_aused")
        s_bhi = sem("s_bhi")
        s_blo = sem("s_blo")
        s_bused = sem("s_bused")
        s_pp = sem("s_pp")
        s_ppa = sem("s_ppa")
        s_ppv = sem("s_ppv")
        s_acc = sem("s_acc")
        s_accfree = sem("s_accfree")
        s_tps = sem("s_tps")
        s_thi = sem("s_thi")
        s_tlo = sem("s_tlo")
        s_qkT = sem("s_qkT")
        s_rows = sem("s_rows")
        s_x = sem("s_x")
        s_sum = sem("s_sum")
        s_nmean = sem("s_nmean")
        s_ss = sem("s_ss")
        s_rstd = sem("s_rstd")
        s_vec = [sem("s_vec0"), sem("s_vec1")]
        s_vecused = sem("s_vecused")
        s_dve = sem("s_dve")
        s_pool = sem("s_pool")
        s_qk = sem("s_qk")
        s_sc = sem("s_sc")
        s_nm = sem("s_nm")
        s_keep = sem("s_keep")
        s_exp = sem("s_exp")
        s_sbw = sem("s_sbw")
        s_comb = sem("s_comb")
        s_pt = sem("s_pt")
        s_pte = sem("s_pte")
        s_pv = sem("s_pv")
        s_o = sem("s_o")
        s_biasl = [sem("s_biasl0"), sem("s_biasl1")]
        s_bias = sem("s_bias")
        s_biasused = sem("s_biasused")
        s_mask = sem("s_mask")
        s_maskused = sem("s_maskused")
        s_nbld = [sem("s_nbld0"), sem("s_nbld1")]
        s_nbst = [sem("s_nbst0"), sem("s_nbst1")]
        s_ext = sem("s_ext")
        s_pw = sem("s_pw")
        s_pla = sem("s_pla")
        s_plb = sem("s_plb")
        s_plc = sem("s_plc")
        s_plo = sem("s_plo")
        s_rt = sem("s_rt")
        s_rhi = sem("s_rhi")
        s_rlo = sem("s_rlo")
        s_rex = sem("s_rex")
        s_rnt = sem("s_rnt")
        s_lam = sem("s_lam")
        s_lamv = sem("s_lamv")
        s_lame = sem("s_lame")
        s_gl = sem("s_gl")
        s_slots = sem("s_slots")
        s_chosen = sem("s_chosen")
        s_place = sem("s_place")
        s_crowd = sem("s_crowd")
        s_xhi = sem("s_xhi")
        s_xlo = sem("s_xlo")
        s_pick = sem("s_pick")
        s_gath = sem("s_gath")
        s_ghi = sem("s_ghi")
        s_glo = sem("s_glo")
        s_ylast = sem("s_ylast")
        s_yhi = sem("s_yhi")
        s_ylo = sem("s_ylo")
        s_scat = sem("s_scat")
        s_merged = sem("s_merged")
        s_out = sem("s_out")

        def row_bcast(ap1d):
            return ap1d.unsqueeze(0).to_broadcast([P, ap1d.shape[0]])

        def gain_rows():
            seq = []
            for i in range(N_LAYERS):
                seq += [a["pool_scale"][i], a["g_mix"][i], a["ln1_g"][i], a["ln1_b"][i], a["ln2_g"][i], a["ln2_b"][i]]
            for l in range(N_LAYERS):
                seq += [a["ffn1_pre_g_2"][l], a["ffn1_post_g_2"][l], a["mix_pre_g_2"][l]]
                seq += [a["b_gate_2"][l, 0], a["b_gate_2"][l, 1], a["diff_subln_g_2"][l], a["b_gate_2"][l, 2]]
                seq += [a["mix_post_g_2"][l], a["ffn2_pre_g_2"][l], a["ffn2_post_g_2"][l]]
            return seq

        GAINS = gain_rows()
        block = ctx.enter_context(nc.Block())

        def wide(w, cols, n=512):
            return w.rearrange("(k p) n -> p k n", p=P)[:, :, cols:cols + n]

        def ffn_walk(eng, experts, a_side, b_side, head, tail, final=False):
            head()
            if experts == 1:
                e = Expert(0, 0)
                turns = (N_FCH - 1) // 2 - final
                with eng.Fori(0, turns) as i:
                    for r in range(2):
                        both(a_side, b_side, Chunk(i, r), e, i * 2 + (r + 1), e, i * 2 + r)
                if final:
                    for r in range(2):
                        both(a_side, b_side, Chunk(turns, r), e, turns * 2 + r + 1, e, turns * 2 + r)
                tail(Chunk((N_FCH - 1) // 2, 0), e, N_FCH - 1)
                return

            def pair(ep, last):
                base = ep * N_FCH
                even, odd = Expert(ep * 2, 0), Expert(ep * 2 + 1, 1)
                for r in range(2):
                    both(a_side, b_side, Chunk(base, r), even, r + 1, even, r)
                with eng.Fori(0, (N_FCH - 3) // 2) as i:
                    for r in range(2):
                        both(a_side, b_side, Chunk(i + base + 1, r), even, i * 2 + (r + 3), even, i * 2 + (r + 2))
                both(a_side, b_side, Chunk(base + 5, 0), odd, 0, even, N_FCH - 1)
                for r in range(2):
                    both(a_side, b_side, Chunk(base + 5, 1 + r), odd, r + 1, odd, r)
                with eng.Fori(0, (N_FCH - 3) // 2) as i:
                    for r in range(2):
                        both(a_side, b_side, Chunk(i + base + 6, 1 + r), odd, i * 2 + (r + 3), odd, i * 2 + (r + 2))
                if not last:
                    both(a_side, b_side, Chunk(base + 10, 1), Expert(ep * 2 + 2, 0), 0, odd, N_FCH - 1)

            with eng.Fori(0, experts // 2 - 1) as ep:
                pair(ep, False)
            pair(experts // 2 - 1, True)
            tail(Chunk((experts // 2) * N_FCH - 1, 1), Expert(experts - 1, 1), N_FCH - 1)

        def is_last(e):
            return isinstance(e.index, int) and e.index == N_EXPERTS - 1

        def both(a_side, b_side, c, ea, ja, eb, jb):
            a_side(c.next(), ea, ja)
            b_side(c, eb, jb)

        @block.sync
        def _(sp):
            n = Tally()
            sp.dma_start(ident[:, :], a["c_ident"]).then_inc(s_xin, 16)
            sp.dma_start(x[:, :, :], a["x"][0].rearrange("(t p) d -> p t d", p=P)).then_inc(s_xin, 16)

            n["b"] = 1

            def weight(src, k, cols):
                slot = n["a"] % 2
                if n["a"] >= 2:
                    sp.wait_ge(s_alo, n["a"] - 1)
                dst = raw_a[:, slot, 0:k * cols].rearrange("p (k n) -> p k n", k=k)
                for j in range(2):
                    sp.dma_start(dst[:, j * k // 2:(j + 1) * k // 2, :], src[:, j * k // 2:(j + 1) * k // 2, :]) \
                      .then_inc(s_al[slot], 16)
                n["a"] += 1

            def gate_up(weights, slot, e, j):
                wg, wu, _, f0u = weights
                for g, (w, f0) in enumerate(((wg, 0), (wu, f0u))):
                    v = w[bass.ds(e * D, D), bass.ds(j * FCH + f0, FCH)]
                    sp.dma_start(raw_a[:, slot, g * 2048:(g + 1) * 2048].rearrange("p (k n) -> p k n", k=KD),
                                 v.rearrange("(k p) n -> p k n", p=P)).then_inc(s_al[slot], 16)

            def first(weights, j):
                sp.wait_ge(s_alo, n["a"] - 1)
                gate_up(weights, n["a"] % 2, 0, j)
                n["a"] += 1

            def ffn(weights, experts, ahead=None):
                a0, b0 = n["a"] - 2, n["b"]

                def side_a(c, e, j):
                    sp.wait_ge(s_alo, c.at(a0 + 1))
                    gate_up(weights, (a0 + c.rest) % 2, e, j)

                def side_b(c, e, j):
                    sp.wait_ge(s_blo, c.at(b0))
                    v = weights[2][bass.ds(e * FF + j * FCH, FCH), :]
                    sp.dma_start(raw_b[:, :].rearrange("p (k n) -> p k n", k=2),
                                 v.rearrange("(k p) n -> p k n", p=P)).then_inc(s_bl, 16)

                def expert(e, half, odd, last):
                    with sp.Fori(0, (N_FCH - 3) // 2) as i:
                        for r in range(2):
                            side_a(Chunk(i + half, odd + r), e, i * 2 + (r + 2))
                            side_b(Chunk(i + half, odd + r), e, i * 2 + r)
                    side_a(Chunk(half + 4, odd), e, N_FCH - 1)
                    side_b(Chunk(half + 4, odd), e, N_FCH - 3)
                    if last:
                        n["a"] = a0 + experts * N_FCH
                    for r in range(2):
                        c = Chunk(half + 4, odd + 1 + r)
                        if not last:
                            side_a(c, e + 1, r)
                        elif ahead:
                            ahead(r)
                        side_b(c, e, N_FCH - 2 + r)

                if experts == 1:
                    expert(0, 0, 0, True)
                else:
                    with sp.Fori(0, experts // 2 - 1) as ep:
                        expert(ep * 2, ep * N_FCH, 0, False)
                        expert(ep * 2 + 1, ep * N_FCH + 5, 1, False)
                    expert(experts - 2, (experts // 2 - 1) * N_FCH, 0, False)
                    expert(experts - 1, (experts // 2 - 1) * N_FCH + 5, 1, True)
                n["b"] += experts * N_FCH

            dense = (a["ffn_wg"][0], a["ffn_wu"][0], a["ffn_wd"][0], 0)
            moe = (a["moe_wg"][0].rearrange("e d f -> (e d) f"), a["moe_wu"][0].rearrange("e d f -> (e d) f"),
                   a["moe_wd"][0].rearrange("e f d -> (e f) d"), 0)
            ffn1 = [(a["ffn1_w_gu_2"][l], a["ffn1_w_gu_2"][l], a["ffn1_w_down_2"][l], FF) for l in range(N_LAYERS)]
            ffn2 = [(a["ffn2_w_gu_2"][l], a["ffn2_w_gu_2"][l], a["ffn2_w_down_2"][l], FF) for l in range(N_LAYERS)]

            for i in range(N_LAYERS):
                for j in range(2 if i else 0, D_IN // 512):
                    weight(wide(a["w_in"][i], 512 * j), KD, 512)
                for j in range(2):
                    weight(wide(a["w_out"][i], 512 * j), KD, 512)
                first((dense, moe)[i], 0)
                first((dense, moe)[i], 1)
                if i == 0:
                    ffn(dense, 1, lambda j: weight(wide(a["w_in"][1], 512 * j), KD, 512))
                else:
                    ffn(moe, N_EXPERTS, lambda j: first(ffn1[0], j))
            for l in range(N_LAYERS):
                w = a["w_in_2"][l]
                ffn(ffn1[l], 1, lambda j: weight(wide(w, (QA, KA)[j]), KD, 512))
                for br, cols in enumerate((((VA, 512),), ((QB, 512), (KB, 256)), ((QC, 512), (KC, 512), (VC, 512)))):
                    for c0, width in cols:
                        weight(wide(w, c0, width), KD, width)
                    for j in range(2):
                        weight(wide(w, GL + 1024 * br + 512 * j), KD, 512)
                    weight(a["w_branch_2"][l, br].rearrange("(k p) n -> p k n", p=P), 4, 1024)
                for j in range(2):
                    weight(wide(a["w_out_2"][l], 512 * j), KD, 512)
                first(ffn2[l], 0)
                first(ffn2[l], 1)
                ffn(ffn2[l], 1, (lambda j: first(ffn1[l + 1], j)) if l + 1 < N_LAYERS else None)
            sp.wait_ge(s_x, 2 * N_LAYERS + 3 * N_LAYERS)
            sp.dma_start(out[0].rearrange("(t p) d -> p t d", p=P), x[:, :, :]).then_inc(s_out, 16)
            sp.wait_ge(s_out, 16)

        @block.tensor
        def _(pe):
            n = Tally()
            bank_free = [None, None]
            pp_free = [None, None]

            def split3(out_ap, l_hi, l_lo, r_hi, r_lo, start, stop):
                nc.tensor.matmul(out_ap, l_hi, r_hi, start=start, stop=False, skip_group_check=True)
                nc.tensor.matmul(out_ap, l_hi, r_lo, start=False, stop=False, skip_group_check=True)
                return nc.tensor.matmul(out_ap, l_lo, r_hi, start=False, stop=stop, skip_group_check=True)

            def group(srcs, value):
                bank = n["g"] % 2
                if bank_free[bank] is not None:
                    pe.wait_ge(*bank_free[bank])
                for dst, src in srcs:
                    mm = nc.tensor.transpose(tp[:, bank, dst:dst + P], src, ident[:, :])
                mm.then_inc(s_tps, 1)
                bank_free[bank] = value
                n["g"] += 1

            def transpose_rows(src, kt):
                for tt in range(TT):
                    n["rows"] += 1
                    pe.wait_ge(s_rows, n["rows"])
                    for g in range(kt // 4):
                        n["lo"] += 1
                        group([(kk * P, src[:, tt, (4 * g + kk) * P:(4 * g + kk + 1) * P]) for kk in range(4)],
                              (s_tlo, n["lo"]))

            def wait_uT():
                pe.wait_ge(s_tlo, n["lo"] - 2)
                n["uT"] = n["lo"]

            def wait_tile(tt):
                if tt == 1 and n["uT"]:
                    pe.wait_ge(s_tlo, n["uT"])
                    n["uT"] = 0

            def take_a():
                n["a"] += 1
                pe.wait_ge(s_alo, n["a"])
                return (n["a"] - 1) % 2

            def wait_pp():
                if n["ppa"]:
                    pe.wait_ge(s_ppa, n["ppa"])
                if n["ppv"]:
                    pe.wait_ge(s_ppv, n["ppv"])

            def project(width=512, gate=False):
                slot = take_a()
                wh = hi_a[:, slot, 0:KD * width].rearrange("p (k n) -> p k n", k=KD)
                wl = lo_a[:, slot, 0:KD * width].rearrange("p (k n) -> p k n", k=KD)
                for tt in range(TT):
                    wait_tile(tt)
                    if pp_free[tt] is not None:
                        pe.wait_ge(*pp_free[tt])
                    for k in range(KD):
                        ts = slice(tt * P, (tt + 1) * P)
                        mm = split3(pp[:, tt, 0:width], uT_hi[:, k, ts], uT_lo[:, k, ts], wh[:, k, :], wl[:, k, :],
                                    k == 0, k == KD - 1)
                    mm.then_inc(s_pp, 1)
                n["pp"] += 2
                n["ppa"] += 2
                n["ppv"] += 2
                pp_free[:] = [(s_ppv, n["ppv"] - 1) if gate else (s_ppa, n["ppa"]), (s_ppv, n["ppv"])]

            def project_out(kt, width, left_hi, left_lo, chunks):
                pe.wait_ge(s_accfree, n["acc"]) if n["acc"] else None
                for j in range(chunks):
                    slot = take_a()
                    wh = hi_a[:, slot, 0:kt * width].rearrange("p (k n) -> p k n", k=kt)
                    wl = lo_a[:, slot, 0:kt * width].rearrange("p (k n) -> p k n", k=kt)
                    for tt in range(TT):
                        wait_tile(tt)
                        for h in range(width // 512):
                            for k in range(kt):
                                ts = slice(tt * P, (tt + 1) * P)
                                cs = slice(h * 512, (h + 1) * 512)
                                mm = split3(acc[:, tt * 2 + j + h, :], left_hi[:, k, ts], left_lo[:, k, ts],
                                            wh[:, k, cs], wl[:, k, cs], k == 0, k == kt - 1)
                    mm.then_inc(s_aused if j + 1 < chunks else s_acc, 1)
                n["acc"] += 1

            n["b"] = 1

            def clear(banks):
                for q in range(banks):
                    nc.tensor.matmul(acc[:, q, :], zeros[:, 0:P], zeros[:, :], start=True, stop=False,
                                     skip_group_check=True)

            def gather(e, count):
                pe.wait_ge(s_pick, count)
                one_hot = pick(e.odd)
                for tt in range(TT):
                    ts = slice(tt * P, (tt + 1) * P)
                    nc.tensor.transpose(pp[:, 1, ts], one_hot[:, ts].bitcast(F32), ident[:, :])
                for k in range(KD):
                    ks = slice(k * P, (k + 1) * P)
                    for tt in range(TT):
                        for part, src in enumerate((x_hi, x_lo)):
                            mm = nc.tensor.matmul(acc[:, 2 + k // 4, (k % 4) * P:(k % 4 + 1) * P],
                                                  src[:, tt, ks],
                                                  one_hot[:, tt * P:(tt + 1) * P],
                                                  start=(tt + part == 0), stop=(tt + part == 2), skip_group_check=True)
                mm.then_inc(s_gath, 1)

            def scatter(tt, bank, odd):
                lhs = put(odd)[:, tt * P:(tt + 1) * P]
                for h in range(2):
                    cs = slice(512 * h, 512 * (h + 1))
                    for part, src in enumerate((y_hi, y_lo)):
                        mm = nc.tensor.matmul(acc[:, bank + h, :], lhs, src[:, cs], start=(part == 0),
                                              stop=(part == 1), skip_group_check=True)
                return mm

            def ffn(experts, final=False, sparse=False):
                a0, b0, g0, lo0, ppv0 = n["a"], n["b"], n["g"], n["lo"], n["ppv"]
                tiles = 1 if sparse else TT
                if n["acc"]:
                    pe.wait_ge(s_accfree, n["acc"])
                clear(2 * tiles)

                def gate_up(c, e, j):
                    slot = (a0 + c.rest) % 2
                    pe.wait_ge(s_alo, c.at(a0 + 1))
                    if c.rest == 0:
                        wait_pp()
                    else:
                        pe.wait_ge(s_ppv, c.half * 4 + (2 * c.rest + ppv0))
                    if sparse and isinstance(j, int) and j == 0:
                        pe.wait_ge(s_glo, e.index + 1)
                    wh = hi_a[:, slot, :].rearrange("p (g k n) -> p g k n", g=2, k=KD)
                    wl = lo_a[:, slot, :].rearrange("p (g k n) -> p g k n", g=2, k=KD)
                    for tt in range(tiles):
                        wait_tile(tt)
                        tile = e.odd if sparse else tt
                        for k in range(KD):
                            ts = slice(tile * P, (tile + 1) * P)
                            mm = split3(pp[:, tt, :], uT_hi[:, k, ts], uT_lo[:, k, ts], wh[:, :, k, :],
                                        wl[:, :, k, :], k == 0, k == KD - 1)
                        mm.then_inc(s_pp, TT // tiles)

                def turn(c):
                    bank = (g0 + c.rest) % 2
                    pe.wait_ge(s_ppv, c.half * 4 + (2 * c.rest + 2 + ppv0))
                    pe.wait_ge(s_tlo, c.at(lo0 - 1))
                    for kk in range(2):
                        for tt in range(tiles):
                            at = (kk * tiles + tt) * P
                            mm = nc.tensor.transpose(tp[:, bank, at:at + P],
                                                     rows[:, tt, FCH + kk * P:FCH + (kk + 1) * P], ident[:, :])
                    mm.then_inc(s_tps, 1)

                def down(c, last):
                    pe.wait_ge(s_blo, c.at(b0 + 1))
                    pe.wait_ge(s_tlo, c.at(lo0 + 1))
                    for kk in range(2):
                        for tt in range(tiles):
                            for h in range(2):
                                at = (kk * tiles + tt) * P
                                ks = slice(at % S, at % S + P)
                                cs = slice(kk * 1024 + h * 512, kk * 1024 + (h + 1) * 512)
                                mm = split3(acc[:, tt * 2 + h, :], hT_hi[:, at // S, ks], hT_lo[:, at // S, ks],
                                            hi_b[:, cs], lo_b[:, cs], False, last and kk == 1)
                    mm.then_inc((s_ylast if sparse else s_acc) if last else s_bused, 1)

                def head():
                    if sparse:
                        pe.wait_ge(s_xlo, 1)
                        gather(Expert(0, 0), 1)
                    gate_up(Chunk(0, 0), Expert(0, 0), 0)
                    turn(Chunk(0, 0))

                def side_b(c, e, j):
                    down(c, False)
                    turn(c.next())
                    if sparse and isinstance(j, int) and j == 1 and not is_last(e):
                        pe.wait_ge(s_merged, e.index * 2 + 1)
                        gather(Expert(None, 1 - e.odd), e.index + 2)
                    if sparse and isinstance(j, int) and j == N_FCH - 1:
                        pe.wait_ge(s_ylo, e.index + 1)
                        clear(2)
                        pe.wait_ge(s_glo, e.index + 2)
                        scatter(0, 2, e.odd).then_inc(s_scat, 1)
                        pe.wait_ge(s_merged, e.index * 2 + 2)
                        scatter(1, 2, e.odd).then_inc(s_scat, 1)

                def tail(c, e, j):
                    down(c, True)
                    if sparse:
                        pe.wait_ge(s_ylo, experts)
                        pe.wait_ge(s_merged, 2 * experts - 1)
                        scatter(0, 2, e.odd).then_inc(s_scat, 1)
                        scatter(1, 0, e.odd).then_inc(s_acc, 1)

                ffn_walk(pe, experts, gate_up, side_b, head, tail, final)
                k = experts * N_FCH
                n["a"] += k
                n["b"] += k
                n["g"] += k
                n["lo"] += k
                n["pp"] += 2 * k
                n["ppa"] += 2 * k
                n["ppv"] += 2 * k
                bank_free[0] = bank_free[1] = (s_tlo, n["lo"])
                pp_free[:] = [(s_ppv, n["ppv"] - 1), (s_ppv, n["ppv"])]
                n["acc"] += 1

            def attention(kind, q0, k0, v0, maps):
                items = maps // 2 if kind == "diff" else maps
                vw = 128 if kind == "diff" else HD
                m0, i0, tq0 = n["map"], n["item"], n["qkT"]

                def pair(p):
                    def cols(base, tt):
                        off = 0 if kind == "sw" and base == k0 else p * P
                        return rows[:, tt, base + off:base + off + P]
                    n["qkT"] += 1
                    group([(b * S + tt * P, cols(base, tt)) for b, base in enumerate((q0, k0)) for tt in range(TT)],
                          (s_qkT, n["qkT"]))

                def qk(m):
                    M = m0 + m
                    if M >= 2:
                        pe.wait_ge(s_sc, M - 1)
                    pe.wait_ge(s_qkT, tq0 + m // 2 + 1)
                    base = (m % 2) * HD
                    src = qkT[base:base + HD, (tq0 + m // 2) % 2, :]
                    for tt in range(TT):
                        mm = nc.tensor.matmul(acc[:, M % 2, tt * S:(tt + 1) * S], src[:, tt * P:(tt + 1) * P],
                                              src[:, S:2 * S], start=True, stop=True)
                    mm.then_inc(s_qk, 1)

                def pt(it):
                    I = i0 + it
                    if I >= 2:
                        pe.wait_ge(s_pte, I - 1)
                    if kind == "diff":
                        pe.wait_ge(s_comb, n["comb"] + it + 1)
                        w = bias[:, it % 2, :, :]
                    else:
                        if kind == "sb":
                            n["sbw"] += 1
                            pe.wait_ge(s_sbw, n["sbw"])
                        else:
                            n["exp"] += 1
                            pe.wait_ge(s_exp, n["exp"])
                        w = sc[:, (m0 + it) % 2, :, :]
                    for kt in range(2):
                        for tt in range(TT):
                            mm = nc.tensor.transpose(acc[:, 2 + I % 2, kt * S + tt * P:kt * S + (tt + 1) * P],
                                                     w[:, tt, kt * P:(kt + 1) * P], ident[:, :])
                    mm.then_inc(s_pt, 1)

                def pv(it):
                    I = i0 + it
                    pe.wait_ge(s_pte, I + 1)
                    if I >= 2:
                        pe.wait_ge(s_o, I - 1)
                    if kind == "sw":
                        vc = v0 + (it % 2) * HD
                    else:
                        vc = v0 + it * vw
                    for tt in range(TT):
                        for kt in range(2):
                            mm = nc.tensor.matmul(pp[:, I % 2, tt * vw:(tt + 1) * vw],
                                                  pT[:, I % 2, kt, tt * P:(tt + 1) * P],
                                                  rows[:, kt, vc:vc + vw], start=(kt == 0), stop=(kt == 1))
                    mm.then_inc(s_pv, 1)

                per = maps // items
                wait_pp()
                if n["acc"]:
                    pe.wait_ge(s_accfree, n["acc"])
                if kind in ("sw", "diff"):
                    n["rows"] += 1
                    pe.wait_ge(s_rows, n["rows"])
                pair(0)
                for m in range(per):
                    qk(m)
                for it in range(items):
                    if per == 2 and it + 1 < items:
                        pair(it + 1)
                    if per == 1 and it % 2 == 0 and it + 2 < items:
                        pair(it // 2 + 1)
                    if it + 1 < items:
                        for m in range(per):
                            qk(per * (it + 1) + m)
                    pt(it)
                    if it >= 1:
                        pv(it - 1)
                pv(items - 1)
                n["map"] += maps
                n["item"] += items
                if kind == "diff":
                    n["comb"] += items
                    n["exp"] += maps
                pe.wait_ge(s_o, n["item"])
                pp_free[:] = [None, None]

            def pooling():
                pe.wait_ge(s_pw, 32 + 16 * n["plc"])
                if n["acc"]:
                    pe.wait_ge(s_accfree, n["acc"])
                wait_pp()
                for g in range(4):
                    for st in range(TT):
                        mm = nc.tensor.matmul(acc[0:64, g // 2, (g % 2) * S:(g % 2 + 1) * S],
                                              rows[:, st, g * 64:(g + 1) * 64],
                                              merged[:, st, g * S:(g + 1) * S], start=(st == 0), stop=(st == 1))
                mm.then_inc(s_pla, 1)
                n["plc"] += 1
                pe.wait_ge(s_plb, n["plc"])
                for tt in range(TT):
                    for g in range(4):
                        mm = nc.tensor.matmul(acc[:, 2 + tt, g * 64:(g + 1) * 64],
                                              pT[0:64, g // 2, g % 2, tt * P:(tt + 1) * P], pool_w[:, g, :],
                                              start=True, stop=True)
                mm.then_inc(s_plc, 1)
                pe.wait_ge(s_plo, n["plc"])

            def router():
                wait_pp()
                pe.wait_ge(s_rlo, 1)
                for tt in range(TT):
                    wait_tile(tt)
                    for k in range(KD):
                        ts = slice(tt * P, (tt + 1) * P)
                        es = slice(k * N_EXPERTS, (k + 1) * N_EXPERTS)
                        mm = split3(pp[:, tt, 0:N_EXPERTS], uT_hi[:, k, ts], uT_lo[:, k, ts], rt_hi[:, es],
                                    rt_lo[:, es], k == 0, k == KD - 1)
                    mm.then_inc(s_pp, 1)
                pe.wait_ge(s_slots, 48)
                pe.wait_ge(s_chosen, 1)
                nc.tensor.matmul(pp[:, 0, 8:16], before_op, chosen[:, 0, :], start=True, stop=True)
                nc.tensor.matmul(pp[:, 1, 8:16], any_op, chosen[:, 0, :], start=True, stop=False)
                nc.tensor.matmul(pp[:, 1, 8:16], before_op, chosen[:, 1, :], start=False, stop=True)
                nc.tensor.matmul(pp[:, 1, 16:24], any_op, chosen[:, 0, :], start=True, stop=False)
                nc.tensor.matmul(pp[:, 1, 16:24], any_op, chosen[:, 1, :], start=False, stop=True) \
                  .then_inc(s_place, 1)
                n["pp"] += 2
                n["ppv"] += 2

            def moe():
                pe.wait_ge(s_crowd, 1)
                full = pe.value_load(crowded[0:1, 0:1], min_val=0, max_val=1)
                start = Tally(n)
                with pe.If(full > 0):
                    ffn(N_EXPERTS)
                n.clear()
                n.update(start)
                with pe.If(full < 1):
                    ffn(N_EXPERTS, sparse=True)

            pe.wait_ge(s_xin, 32)
            pe.wait_ge(s_zero, 3)
            pe.sem_inc(s_bused, 1)
            for i in range(N_LAYERS):
                transpose_rows(x, KD)
                wait_uT()
                for j in range(D_IN // 512):
                    project()
                pooling()
                attention("chunk", 256, 640, 1024, CHUNK_HEADS)
                attention("sb", 1408, 1792, 2176, SB_HEADS)
                transpose_rows(t, KD)
                wait_uT()
                project_out(KD, 512, uT_hi, uT_lo, 2)
                transpose_rows(x, KD)
                wait_uT()
                if i == 1:
                    router()
                    moe()
                else:
                    ffn(1)
            for l in range(N_LAYERS):
                transpose_rows(t, KD)
                wait_uT()
                ffn(1)
                transpose_rows(t, KD)
                wait_uT()
                for kind, q0, k0, v0, maps, widths in (("na", 0, 512, 1024, 8, (512, 512, 512)),
                                                       ("sw", 1024, 512, 640, 8, (512, 256)),
                                                       ("diff", 0, 512, 1024, 8, (512, 512, 512))):
                    for width in widths:
                        project(width)
                    attention(kind, q0, k0, v0, maps)
                    project(gate=True)
                    transpose_rows(rows, 4)
                    turned = n["lo"]
                    project(gate=True)
                    pe.wait_ge(s_tlo, turned)
                    project_out(4, 1024, hT_hi, hT_lo, 1)
                transpose_rows(merged, KD)
                wait_uT()
                project_out(KD, 512, uT_hi, uT_lo, 2)
                transpose_rows(t, KD)
                wait_uT()
                ffn(1, l + 1 == N_LAYERS)

        @block.scalar
        def _(act):
            n = Tally()
            landed = [0, 0]
            n["b"] = n["bu"] = 1

            def hi_chunk_a(freed=None):
                slot = n["a"] % 2
                landed[slot] += 32
                act.wait_ge(s_al[slot], landed[slot])
                if freed:
                    act.wait_ge(*freed)
                nc.scalar.activation(hi_a[:, slot, :], raw_a[:, slot, :], ACT.Copy).then_inc(s_ahi, 1)
                n["a"] += 1

            def hi_groups(dst, groups):
                for tt in range(TT):
                    for g in range(groups):
                        n["g"] += 1
                        act.wait_ge(s_tps, n["g"])
                        nc.scalar.activation(dst[:, 4 * g:4 * g + 4, tt * P:(tt + 1) * P],
                                             tp[:, (n["g"] - 1) % 2, :].rearrange("p (k s) -> p k s", k=4),
                                             ACT.Copy).then_inc(s_thi, 1)

            def project_copy(c0, width=512):
                act.wait_ge(s_pp, n["pp"] + 1)
                nc.scalar.activation(rows[:, 0, c0:c0 + width], pp[:, 0, 0:width], ACT.Copy).then_inc(s_ppa, 2)
                n["pp"] += 2
                hi_chunk_a((s_pp, n["pp"]))

            def out_chunk(last):
                if last:
                    hi_chunk_a((s_acc, n["acc"] + 1))
                else:
                    n["aused"] += 1
                    hi_chunk_a((s_aused, n["aused"]))

            def gathered(odd, count):
                act.wait_ge(s_gath, count)
                nc.scalar.activation(put(odd), pp[:, 1, 0:S], ACT.Copy)
                nc.scalar.activation(uT_hi[:, :, odd * P:(odd + 1) * P].rearrange("p (b k) s -> p b k s", b=2),
                                     acc[:, 2:4, :].rearrange("p b (k s) -> p b k s", s=P), ACT.Copy) \
                  .then_inc(s_ghi, 1)

            def split_y():
                nc.scalar.activation(y_hi[:, :].rearrange("p (h c) -> p h c", h=2), acc[:, 0:2, :],
                                     ACT.Copy).then_inc(s_yhi, 1)

            def ffn(experts, final=False, sparse=False):
                a1, b0, g0, pp0, bu0 = n["a"], n["b"], n["g"], n["pp"], n["bu"]
                tiles = 1 if sparse else TT
                last = experts * N_FCH - 1
                base = list(landed)

                def hi_next(c, part):
                    if final and isinstance(c.half, int) and c.at(0) >= last - 1:
                        return
                    slot = (a1 + c.rest) % 2
                    if part == 0:
                        act.wait_ge(s_al[slot], c.turns(0) * 32 + (base[slot] + 32))
                    cs = slice(part * 2048, (part + 1) * 2048)
                    nc.scalar.activation(hi_a[:, slot, cs], raw_a[:, slot, cs], ACT.Copy) \
                      .then_inc((s_ahalf, s_ahi)[part], 1)

                def silu(c):
                    for tt in range(tiles):
                        act.wait_ge(s_pp, c.half * 4 + (2 * c.rest + tt + 1 + TT - tiles + pp0))
                        nc.scalar.activation(rows[:, tt, 0:FCH], pp[:, tt, 0:FCH], ACT.Silu) \
                          .then_inc(s_ppa, TT // tiles)

                def down_side(c):
                    act.wait_ge(s_tps, c.at(g0 + 1))
                    nc.scalar.activation(hT_hi[:, 0:tiles, :].rearrange("p k s -> p (k s)"),
                                         tp[:, (g0 + c.rest) % 2, 0:tiles * S], ACT.Copy).then_inc(s_thi, 1)
                    act.wait_ge(s_bl, c.half * 32 + 16 * (c.rest + b0))
                    act.wait_ge(s_bused, c.at(bu0))
                    nc.scalar.activation(hi_b[:, :], raw_b[:, :], ACT.Copy).then_inc(s_bhi, 1)

                def head():
                    if sparse:
                        nc.scalar.activation(x_hi[:, :, :], x[:, :, :], ACT.Copy).then_inc(s_xhi, 1)
                        gathered(0, 1)
                    body(Chunk(0, 0), Expert(0, 0), None)

                def body(c, e, j):
                    silu(c)
                    hi_next(c, 0)
                    if sparse and isinstance(j, int) and j == 0:
                        act.wait_ge(s_bused, c.at(bu0))
                        split_y()
                    down_side(c)
                    hi_next(c, 1)
                    if sparse and isinstance(j, int) and j == 2 and not is_last(e):
                        gathered(1 - e.odd, e.index + 2)

                def tail(c, e, j):
                    if sparse:
                        act.wait_ge(s_ylast, 1)
                        split_y()

                ffn_walk(act, experts, body, lambda c, e, j: None, head, tail, final)
                k = experts * N_FCH
                for c in range(k):
                    landed[(a1 + c) % 2] += 32
                n["bu"] += k - 1
                n["a"] += k
                n["b"] += k
                n["g"] += k
                n["pp"] += 2 * k

            def squares(srcs, final=None):
                for k, (src, col, b) in enumerate(srcs):
                    w = 1
                    for d in src.shape[1:]:
                        w *= d
                    scratch = sc[:, :, :, :].rearrange("p s t k -> p (s t k)")[:, 0:w]
                    if len(src.shape) == 3:
                        scratch = scratch.rearrange("p (a b) -> p a b", a=src.shape[1])
                    if n["ss"]:
                        act.wait_ge(s_ss, n["ss"])
                    nc.scalar.activation(scratch, src, ACT.Square, bias=b, accum_out=ss[:, col:col + 1]) \
                      .then_inc(s_ss, 1)
                    n["ss"] += 1

            def soft_exp(m, kind):
                M = n["m0"] + m
                n["nm"] += 1
                act.wait_ge(s_nm, n["nm"])
                for tt in range(TT):
                    last = nc.scalar.activation(sc[:, M % 2, tt, :], sc[:, M % 2, tt, :], ACT.Exp,
                                                bias=negmax[:, M % 4, tt:tt + 1],
                                                accum_out=psums[:, M % 4, tt:tt + 1])
                if kind == "sw":
                    h = m // 2 + 4 * (m % 2)
                    last = nc.scalar.activation(esink[:, M % 4, :], negmax[:, M % 4, :], ACT.Exp,
                                                bias=sink[:, h:h + 1])
                last.then_inc(s_exp, 1)

            def sb_sigmoids(m):
                M = n["m0"] + m
                act.wait_ge(s_sc, M + 1)
                z = sc[:, M % 2, :, :]
                nc.scalar.activation(bias[:, m % 2, :, :], z, ACT.Sigmoid, scale=-1.0)
                nc.scalar.activation(z, z, ACT.Sigmoid).then_inc(s_keep, 1)

            def attention(kind, maps):
                items = maps // 2 if kind == "diff" else maps
                per = maps // items
                n["m0"], n["i0"] = n["map"], n["item"]

                def pair():
                    n["g"] += 1
                    act.wait_ge(s_tps, n["g"])
                    nc.scalar.activation(qkT[:, n["qkT"] % 2, :], tp[:, (n["g"] - 1) % 2, :], ACT.Copy) \
                      .then_inc(s_qkT, 1)
                    n["qkT"] += 1

                def soften(m):
                    if kind == "sb":
                        sb_sigmoids(m)
                    else:
                        soft_exp(m, kind)

                def copy_pT(it):
                    I = n["i0"] + it
                    act.wait_ge(s_pt, I + 1)
                    if I >= 2:
                        act.wait_ge(s_pv, I - 1)
                    nc.scalar.activation(pT[:, I % 2, :, :].rearrange("p k s -> p (k s)"), acc[:, 2 + I % 2, :],
                                         ACT.Copy).then_inc(s_pte, 1)

                pair()
                for m in range(per):
                    soften(m)
                for it in range(items):
                    if per == 2 and it + 1 < items:
                        pair()
                    if per == 1 and it % 2 == 0 and it + 2 < items:
                        pair()
                    copy_pT(it)
                    if it + 1 < items:
                        for m in range(per):
                            soften(per * (it + 1) + m)
                n["map"] += maps
                n["item"] += items

            def wait_nmean():
                n["nmean"] += 1
                act.wait_ge(s_nmean, n["nmean"])

            act.wait_ge(s_zero, 3)
            for i in range(N_LAYERS):
                hi_groups(uT_hi, 2)
                if i == 0:
                    hi_chunk_a()
                    hi_chunk_a()
                    act.wait_ge(s_rt, 16)
                    nc.scalar.activation(rt_hi[:, :], rt[:, :], ACT.Copy).then_inc(s_rhi, 1)
                    act.wait_ge(s_ext, 64)
                for j in range(D_IN // 512):
                    project_copy(512 * j)
                attention("chunk", CHUNK_HEADS)
                attention("sb", SB_HEADS)
                act.wait_ge(s_o, n["item"])
                squares([(t[:, tt, c0:c1], tt * 3 + k, 0.0) for tt in range(TT)
                         for k, (c0, c1) in enumerate(((0, 256), (256, 640), (640, 1024)))])
                hi_groups(uT_hi, 2)
                out_chunk(False)
                wait_nmean()
                squares([(x[:, tt, :], tt, nmean[:, tt:tt + 1]) for tt in range(TT)])
                hi_groups(uT_hi, 2)
                out_chunk(True)
                n["acc"] += 1
                if i == 1:
                    act.wait_ge(s_rnt, 1)
                    nc.scalar.activation(logit[:, :, :], logit[:, :, :], ACT.Exp).then_inc(s_rex, 1)
                    n["pp"] += 2
                    act.wait_ge(s_crowd, 1)
                    full = act.value_load(crowded[0:1, 0:1], min_val=0, max_val=1)
                    start, landed_start = Tally(n), list(landed)
                    with act.If(full > 0):
                        ffn(N_EXPERTS)
                    n.clear()
                    n.update(start)
                    landed[:] = landed_start
                    with act.If(full < 1):
                        ffn(N_EXPERTS, sparse=True)
                else:
                    ffn(1)
                n["acc"] += 1
                wait_nmean()
                squares([(x[:, tt, :], tt, nmean[:, tt:tt + 1]) for tt in range(TT)])
                n["x"] += 2
            for l in range(N_LAYERS):
                def pre():
                    act.wait_ge(s_x, n["x"])
                    squares([(x[:, tt, :], tt, 0.0) for tt in range(TT)])
                    hi_groups(uT_hi, 2)

                def post():
                    n["acc"] += 1
                    act.wait_ge(s_acc, n["acc"])
                    squares([(acc[:, 2 * tt:2 * tt + 2, :], tt, 0.0) for tt in range(TT)])
                    n["x"] += 1

                pre()
                act.wait_ge(s_lamv, l + 1)
                nc.scalar.activation(lam_e[:, :], lam_s[:, :], ACT.Exp).then_inc(s_lame, 1)
                ffn(1)
                post()
                pre()
                for br, (kind, cols) in enumerate((("na", ((0, 512), (512, 512), (1024, 512))),
                                                   ("sw", ((0, 512), (512, 256))),
                                                   ("diff", ((0, 512), (512, 512), (1024, 512))))):
                    for c0, width in cols:
                        project_copy(c0, width)
                    attention(kind, 8)
                    for j in range(2):
                        n["pp"] += 2
                        n["gl"] += 1
                        act.wait_ge(s_gl, n["gl"])
                        g = rows[:, :, 1536 + 512 * j:2048 + 512 * j]
                        nc.scalar.activation(g, g, ACT.Sigmoid).then_inc(s_ppa, 2)
                        hi_chunk_a((s_pp, n["pp"]))
                        if j == 0:
                            hi_groups(hT_hi, 1)
                    out_chunk(True)
                    n["acc"] += 1
                hi_groups(uT_hi, 2)
                out_chunk(False)
                post()
                n["acc"] -= 1
                pre()
                out_chunk(True)
                n["acc"] += 1
                ffn(1, l + 1 == N_LAYERS)
                post()

        @block.vector
        def _(dve):
            n = Tally()

            def link(ins):
                n["dve"] += 1
                ins.then_inc(s_dve, 1)
                dve.wait_ge(s_dve, n["dve"])

            def signal(s):
                dve.sem_inc(s, 1)

            def lo_chunk_a():
                slot = n["a"] % 2
                n["a"] += 1
                dve.wait_ge(s_ahi, n["a"])
                nc.vector.tensor_tensor(lo_a[:, slot, :], raw_a[:, slot, :], hi_a[:, slot, :].bitcast(F32),
                                        ALU.subtract).then_inc(s_alo, 1)

            def lo_groups(hi, lo, groups):
                for tt in range(TT):
                    for g in range(groups):
                        n["g"] += 1
                        n["thi"] += 1
                        dve.wait_ge(s_thi, n["thi"])
                        ks, ts = slice(4 * g, 4 * g + 4), slice(tt * P, (tt + 1) * P)
                        nc.vector.tensor_tensor(lo[:, ks, ts],
                                                tp[:, (n["g"] - 1) % 2, :].rearrange("p (k s) -> p k s", k=4),
                                                hi[:, ks, ts].bitcast(F32), ALU.subtract).then_inc(s_tlo, 1)

            def project_copy(c0, width=512, split=True):
                n["pp"] += 2
                dve.wait_ge(s_pp, n["pp"])
                nc.vector.tensor_copy(rows[:, 1, c0:c0 + width], pp[:, 1, 0:width]).then_inc(s_ppv, 2)
                if split:
                    lo_chunk_a()

            def gain():
                slot = n["vec"] % 2
                dve.wait_ge(s_vec[slot], 16 * (n["vec"] // 2 + 1))
                n["vec"] += 1
                return slot

            def wait_rstd():
                n["rstd"] += 1
                dve.wait_ge(s_rstd, n["rstd"])

            def write_pick(e, count):
                for tt in range(TT):
                    ins = nc.vector.tensor_scalar(pick(e.odd)[:, tt * P:(tt + 1) * P], slot_ids,
                                                  slot_of[:, tt, bass.ds(count, 1)], None, ALU.is_equal)
                ins.then_inc(s_pick, 1)

            def gathered(odd, count):
                dve.wait_ge(s_ghi, count)
                us = uT_hi[:, :, odd * P:(odd + 1) * P].rearrange("p (b k) s -> p b k s", b=2).bitcast(F32)
                nc.vector.tensor_tensor(uT_lo[:, :, odd * P:(odd + 1) * P].rearrange("p (b k) s -> p b k s", b=2),
                                        acc[:, 2:4, :].rearrange("p b (k s) -> p b k s", s=P), us, ALU.subtract) \
                  .then_inc(s_glo, 1)

            def split_y(count):
                dve.wait_ge(s_yhi, count)
                nc.vector.tensor_tensor(y_lo[:, :].rearrange("p (h c) -> p h c", h=2), acc[:, 0:2, :],
                                        y_hi[:, :].rearrange("p (h c) -> p h c", h=2).bitcast(F32), ALU.subtract).then_inc(s_ylo, 1)

            def merge(tt, bank, e):
                dve.wait_ge(s_merged, e * 2 + 1)
                o = merged[:, tt, :].rearrange("p (h c) -> p h c", h=2)
                nc.vector.scalar_tensor_tensor(out=o, in0=acc[:, bank:bank + 2, :],
                                               scalar=gates[:, tt, bass.ds(e, 1)], in1=o, op0=ALU.mult,
                                               op1=ALU.add).then_inc(s_merged, 1)

            def ffn(experts, final=False, sparse=False):
                a1, b0, g0, hi0, ppa0, half0 = n["a"], n["b"], n["g"], n["thi"], n["ppa"], n["half"]
                tiles = 1 if sparse else TT

                def lo_next(c, part):
                    if final and isinstance(c.half, int) and c.at(0) >= N_FCH - 2:
                        return
                    slot = (a1 + c.rest) % 2
                    dve.wait_ge((s_ahalf, s_ahi)[part], c.at((half0, a1)[part] + 1))
                    cs = slice(part * 2048, (part + 1) * 2048)
                    ins = nc.vector.tensor_tensor(lo_a[:, slot, cs], raw_a[:, slot, cs],
                                                  hi_a[:, slot, cs].bitcast(F32), ALU.subtract)
                    if part:
                        ins.then_inc(s_alo, 1)

                def hidden(c, e):
                    for tt in range(tiles):
                        dve.wait_ge(s_ppa, c.half * 4 + (2 * c.rest + tt + 1 + TT - tiles + ppa0))
                        o, s, u = rows[:, tt, FCH:2 * FCH], rows[:, tt, 0:FCH], pp[:, tt, FCH:2 * FCH]
                        if experts == 1 or sparse:
                            ins = nc.vector.tensor_tensor(o, s, u, ALU.mult)
                        else:
                            ins = nc.vector.scalar_tensor_tensor(out=o, in0=s,
                                                                 scalar=gates[:, tt, bass.ds(e.index, 1)],
                                                                 in1=u, op0=ALU.mult, op1=ALU.mult)
                        ins.then_inc(s_ppv, TT // tiles)

                def turned(c):
                    dve.wait_ge(s_thi, c.at(hi0 + 1))
                    nc.vector.tensor_tensor(hT_lo[:, 0:tiles, :].rearrange("p k s -> p (k s)"),
                                            tp[:, (g0 + c.rest) % 2, 0:tiles * S],
                                            hT_hi[:, 0:tiles, :].rearrange("p k s -> p (k s)").bitcast(F32),
                                            ALU.subtract).then_inc(s_tlo, 1)

                def lo_b_rows(c):
                    dve.wait_ge(s_bhi, c.at(b0 + 1))
                    nc.vector.tensor_tensor(lo_b[:, :], raw_b[:, :], hi_b[:, :].bitcast(F32),
                                            ALU.subtract).then_inc(s_blo, 1)

                def head():
                    if sparse:
                        nc.vector.memset(merged[:, :, :], 0.0).then_inc(s_merged, 1)
                        dve.wait_ge(s_slots, 48)
                        write_pick(Expert(0, 0), 0)
                        dve.wait_ge(s_xhi, 1)
                        nc.vector.tensor_tensor(x_lo[:, :, :], x[:, :, :], x_hi[:, :, :].bitcast(F32), ALU.subtract) \
                          .then_inc(s_xlo, 1)
                        gathered(0, 1)
                    body(Chunk(0, 0), Expert(0, 0), None)

                def merge_before(tt, e):
                    dve.wait_ge(s_scat, e.index * 2 + (tt - 1))
                    merge(tt, 2, e.index - 1)

                def body(c, e, j):
                    ended = sparse and isinstance(j, int) and j == 0
                    hidden(c, e)
                    lo_next(c, 0)
                    if ended:
                        split_y(e.index)
                    turned(c)
                    if ended:
                        merge_before(0, e)
                    lo_b_rows(c)
                    if ended:
                        merge_before(1, e)
                    lo_next(c, 1)
                    if sparse and isinstance(j, int) and not is_last(e):
                        if j == 1:
                            write_pick(Expert(None, 1 - e.odd), e.index + 1)
                        if j == 2:
                            gathered(1 - e.odd, e.index + 2)

                def tail(c, e, j):
                    if sparse:
                        split_y(experts)
                        dve.wait_ge(s_scat, 2 * experts - 1)
                        merge(0, 2, experts - 1)
                        dve.wait_ge(s_acc, n["acc"] + 1)
                        merge(1, 0, experts - 1)
                        dve.wait_ge(s_merged, 2 * experts + 1)

                ffn_walk(dve, experts, body, lambda c, e, j: None, head, tail, final)
                k = experts * N_FCH
                n["a"] += k
                n["half"] += k
                n["b"] += k
                n["g"] += k
                n["thi"] += k
                n["pp"] += 2 * k
                n["ppa"] += 2 * k

            def residual(sparse=False):
                n["acc"] += 1
                dve.wait_ge(s_acc, n["acc"])
                for tt in range(TT):
                    y = merged[:, tt, :].rearrange("p (h c) -> p h c", h=2) if sparse else acc[:, 2 * tt:2 * tt + 2, :]
                    link(nc.vector.scalar_tensor_tensor(out=x[:, tt, :].rearrange("p (h c) -> p h c", h=2),
                                                        in0=x[:, tt, :].rearrange("p (h c) -> p h c", h=2),
                                                        scalar=ALPHA, in1=y, op0=ALU.mult, op1=ALU.add,
                                                        accum_out=sm[:, tt:tt + 1]))

            def layer_norm(turned=True):
                signal(s_sum)
                signal(s_accfree)
                wait_rstd()
                g, b = gain(), gain()
                for tt in range(TT):
                    link(nc.vector.tensor_scalar(x[:, tt, :], x[:, tt, :], nmean[:, tt:tt + 1], rstd[:, tt:tt + 1],
                                                 ALU.add, ALU.mult))
                    link(nc.vector.tensor_tensor(x[:, tt, :], x[:, tt, :], vec[:, g, :], ALU.mult))
                    link(nc.vector.tensor_tensor(x[:, tt, :], x[:, tt, :], vec[:, b, :], ALU.add))
                    if turned:
                        signal(s_rows)
                signal(s_vecused)
                signal(s_vecused)
                signal(s_x)

            def attention(kind, maps, dst, width):
                items = maps // 2 if kind == "diff" else maps
                per = maps // items
                m0, i0 = n["map"], n["item"]
                biased = kind in ("chunk", "na")

                def scores(m):
                    M = m0 + m
                    dve.wait_ge(s_qk, M + 1)
                    if kind != "diff":
                        if i0 + m >= 2:
                            dve.wait_ge(s_pt, i0 + m - 1)
                    s_in, s_o_ = acc[:, M % 2, :].rearrange("p (t k) -> p t k", t=TT), sc[:, M % 2, :, :]
                    if biased:
                        n["bias"] += 1
                        dve.wait_ge(s_bias, n["bias"])
                        add = bias[:, (n["bias"] - 1) % 2, :, ::-1]
                    else:
                        add = mask[:, :, :]
                    if kind == "diff":
                        ins = nc.vector.tensor_scalar(s_o_, s_in, SCALE, None, ALU.mult)
                    else:
                        ins = nc.vector.scalar_tensor_tensor(out=s_o_, in0=s_in, scalar=SCALE, in1=add, op0=ALU.mult,
                                                             op1=ALU.add)
                    link(ins)
                    signal(s_sc)
                    if biased:
                        signal(s_biasused)
                    if kind == "sb":
                        return
                    if kind == "sw":
                        h = m // 2 + 4 * (m % 2)
                        link(nc.vector.tensor_reduce(negmax[:, M % 4, :], s_o_, AX_X, ALU.max, negate=True))
                        nc.vector.tensor_scalar(negmax[:, M % 4, :], negmax[:, M % 4, :], nsink[:, h:h + 1], None,
                                                ALU.min).then_inc(s_nm, 1)
                    else:
                        nc.vector.tensor_reduce(negmax[:, M % 4, :], s_o_, AX_X, ALU.max, negate=True) \
                          .then_inc(s_nm, 1)

                def stick(m):
                    M = m0 + m
                    keep, w = bias[:, m % 2, :, :], sc[:, M % 2, :, :]
                    n["keep"] += 1
                    dve.wait_ge(s_keep, n["keep"])
                    for tt in range(TT):
                        ins = nc.vector.tensor_tensor_scan(keep[:, tt, ::-1], keep[:, tt, ::-1],
                                                           zcol.to_broadcast([P, S]), 1.0, ALU.mult, ALU.add)
                        if tt:
                            link(ins)
                    nc.vector.tensor_tensor(w[:, :, 0:S - 1], w[:, :, 0:S - 1], keep[:, :, 1:S], ALU.mult) \
                      .then_inc(s_sbw, 1)

                def combine(it):
                    M = m0 + 2 * it
                    dve.wait_ge(s_exp, n["exp"] + 2 * it + 2)
                    if i0 + it >= 2:
                        dve.wait_ge(s_pt, i0 + it - 1)
                    for k in range(2):
                        link(nc.vector.reciprocal(rsum[:, (M + k) % 4, :], psums[:, (M + k) % 4, :]))
                    link(nc.vector.tensor_scalar(rsum[:, (M + 1) % 4, :], rsum[:, (M + 1) % 4, :], nlam, None,
                                                 ALU.mult))
                    for tt in range(TT):
                        w = bias[:, it % 2, tt, :]
                        link(nc.vector.tensor_scalar(w, sc[:, M % 2, tt, :], rsum[:, M % 4, tt:tt + 1], None,
                                                     ALU.mult))
                        link(nc.vector.scalar_tensor_tensor(out=w, in0=sc[:, (M + 1) % 2, tt, :],
                                                            scalar=rsum[:, (M + 1) % 4, tt:tt + 1], in1=w,
                                                            op0=ALU.mult, op1=ALU.add))
                    signal(s_comb)

                def output(it):
                    I, M = i0 + it, m0 + it
                    dve.wait_ge(s_pv, I + 1)
                    vw = 128 if kind == "diff" else HD
                    if kind == "sw":
                        h = it // 2 + 4 * (it % 2)
                    else:
                        h = it
                    src = pp[:, I % 2, 0:2 * vw].rearrange("p (t d) -> p t d", t=TT)
                    o = dst[:, :, h * vw:(h + 1) * vw]
                    if kind in ("sb", "diff"):
                        ins = nc.vector.tensor_copy(o, src)
                    else:
                        if kind == "sw":
                            link(nc.vector.tensor_tensor(psums[:, M % 4, :], psums[:, M % 4, :], esink[:, M % 4, :],
                                                         ALU.add))
                        link(nc.vector.reciprocal(rsum[:, M % 4, :], psums[:, M % 4, :]))
                        ins = nc.vector.tensor_tensor(o, src, rsum[:, M % 4, :].unsqueeze(2).to_broadcast([P, TT, vw]),
                                                      ALU.mult)
                    ins.then_inc(s_o, 1)

                if not biased and kind != "diff":
                    dve.wait_ge(s_mask, 16 * mask_index[kind][n["layer"]])
                for m in range(per):
                    scores(m)
                if kind == "diff":
                    combine(0)
                if kind == "sb":
                    stick(0)
                for it in range(items):
                    if it + 1 < items:
                        for m in range(per):
                            scores(per * (it + 1) + m)
                        if kind == "diff":
                            combine(it + 1)
                    if it >= 1:
                        output(it - 1)
                    if kind == "sb" and it + 1 < items:
                        stick(it + 1)
                output(items - 1)
                if kind != "sb":
                    n["exp"] += maps
                n["map"] += maps
                n["item"] += items
                dve.wait_ge(s_o, n["item"])
                if kind in ("sb", "sw"):
                    signal(s_maskused)

            mask_index = {"sb": (2, 4), "sw": (6, 8)}

            def rotate(h0, h1, regroup):
                heads = h1 - h0
                for tt in range(TT):
                    v = rows[:, tt, h0 * HD:h1 * HD].rearrange("p (h d) -> p h d", d=HD)
                    w = t[:, tt, h0 * HD:h1 * HD].rearrange("p (h d) -> p h d", d=HD)
                    for half in range(2):
                        o = slice(32 * half, 32 * half + 32)
                        i_ = slice(32 - 32 * half, 64 - 32 * half)
                        ins = nc.vector.tensor_tensor(w[:, :, o], v[:, :, i_],
                                                      rope[:, 1, tt, o].unsqueeze(1).to_broadcast([P, heads, 32]),
                                                      ALU.mult)
                        if half:
                            link(ins)
                    link(nc.vector.tensor_tensor(v, v, rope[:, 0, tt, :].unsqueeze(1).to_broadcast([P, heads, HD]),
                                                 ALU.mult))
                    if regroup:
                        link(nc.vector.tensor_tensor(
                            rows[:, tt, 1024:1536].rearrange("p (q a d) -> p a q d", a=2, d=HD),
                            v.rearrange("p (a q) d -> p a q d", a=2), w.rearrange("p (a q) d -> p a q d", a=2),
                            ALU.add))
                    else:
                        link(nc.vector.tensor_tensor(v, v, w, ALU.add))

            nc.vector.memset(zeros[:, :], 0.0).then_inc(s_zero, 1)
            nc.vector.memset(stat[:, :], 0.0).then_inc(s_zero, 1)
            dve.wait_ge(s_zero, 2)
            nc.vector.memset(half_pow, -0.5).then_inc(s_zero, 1)
            dve.wait_ge(s_zero, 3)
            dve.wait_ge(s_xin, 32)
            signal(s_rows)
            signal(s_rows)
            signal(s_blo)

            for i in range(N_LAYERS):
                n["layer"] = i
                lo_groups(uT_hi, uT_lo, 2)
                if i == 0:
                    lo_chunk_a()
                    lo_chunk_a()
                    dve.wait_ge(s_rhi, 1)
                    nc.vector.tensor_tensor(rt_lo[:, :], rt[:, :], rt_hi[:, :].bitcast(F32), ALU.subtract) \
                      .then_inc(s_rlo, 1)
                    dve.wait_ge(s_const, 32)
                    dve.wait_ge(s_ext, 64)
                for j in range(D_IN // 512):
                    project_copy(512 * j)
                n["ppa"] += 10
                dve.wait_ge(s_pla, i + 1)
                nc.vector.tensor_copy(pT[0:64, :, :, :].rearrange("p a b s -> p (a b s)"),
                                      acc[0:64, 0:2, :].rearrange("p a s -> p (a s)")).then_inc(s_plb, 1)
                slot = gain()
                dve.wait_ge(s_plc, i + 1)
                for tt in range(TT):
                    link(nc.vector.tensor_tensor(t[:, tt, 0:D_POOL], acc[:, 2 + tt, 0:D_POOL], vec[:, slot, 0:D_POOL],
                                                 ALU.mult))
                signal(s_vecused)
                signal(s_plo)
                n["g"] += 3
                attention("chunk", CHUNK_HEADS, t[:, :, 256:640], 384)
                n["g"] += 3
                attention("sb", SB_HEADS, t[:, :, 640:1024], 384)
                wait_rstd()
                slot = gain()
                for tt in range(TT):
                    for k, (c0, c1) in enumerate(((0, 256), (256, 640), (640, 1024))):
                        link(nc.vector.scalar_tensor_tensor(out=t[:, tt, c0:c1], in0=t[:, tt, c0:c1],
                                                            scalar=rstd[:, tt * 3 + k:tt * 3 + k + 1],
                                                            in1=vec[:, slot, c0:c1], op0=ALU.mult, op1=ALU.mult))
                    signal(s_rows)
                signal(s_vecused)
                lo_groups(uT_hi, uT_lo, 2)
                lo_chunk_a()
                residual()
                layer_norm()
                lo_groups(uT_hi, uT_lo, 2)
                lo_chunk_a()
                if i == 1:
                    n["pp"] += 2
                    dve.wait_ge(s_pp, n["pp"])
                    for tt in range(TT):
                        link(nc.vector.tensor_copy(logit[:, tt, :], pp[:, tt, 0:8]))
                    for tt in range(TT):
                        lj = logit[:, tt, :].unsqueeze(1).to_broadcast([P, 8, 8])
                        le = logit[:, tt, :].unsqueeze(2).to_broadcast([P, 8, 8])
                        c1v = cmp1[:, :].rearrange("p (e j) -> p e j", e=8)
                        c2v = cmp2[:, :].rearrange("p (e j) -> p e j", e=8)
                        link(nc.vector.tensor_tensor(c1v, lj, le, ALU.is_gt))
                        link(nc.vector.tensor_tensor(c2v, lj, le, ALU.is_equal))
                        link(nc.vector.tensor_tensor(cmp2[:, :], cmp2[:, :], earlier[:, :], ALU.mult))
                        link(nc.vector.tensor_tensor(cmp1[:, :], cmp1[:, :], cmp2[:, :], ALU.add))
                        link(nc.vector.tensor_reduce(rank, c1v, AX_X, ALU.add))
                        link(nc.vector.tensor_scalar(chosen[:, tt, :], rank, 2.0, None, ALU.is_lt))
                        link(nc.vector.tensor_reduce(top[:, tt:tt + 1], logit[:, tt, :], AX_X, ALU.max))
                        link(nc.vector.tensor_scalar(logit[:, tt, :], logit[:, tt, :], top[:, tt:tt + 1], None,
                                                     ALU.subtract))
                    signal(s_chosen)
                    signal(s_rnt)
                    dve.wait_ge(s_rex, 1)
                    for tt in range(TT):
                        link(nc.vector.tensor_tensor(gates[:, tt, :], chosen[:, tt, :], logit[:, tt, :], ALU.mult))
                        link(nc.vector.tensor_reduce(gsum[:, tt:tt + 1], gates[:, tt, :], AX_X, ALU.add))
                        link(nc.vector.reciprocal(gsum[:, tt:tt + 1], gsum[:, tt:tt + 1]))
                        link(nc.vector.tensor_scalar(gates[:, tt, :], gates[:, tt, :], gsum[:, tt:tt + 1], None,
                                                     ALU.mult))
                    dve.wait_ge(s_place, 1)
                    for tt in range(TT):
                        link(nc.vector.scalar_tensor_tensor(out=slot_of[:, tt, :], in0=pp[:, tt, 8:16], scalar=1.0,
                                                            in1=chosen[:, tt, :], op0=ALU.add, op1=ALU.mult))
                        link(nc.vector.tensor_scalar(slot_of[:, tt, :], slot_of[:, tt, :], -1.0, None, ALU.add))
                    link(nc.vector.tensor_reduce(most, pp[:, 1, 16:24], AX_X, ALU.max))
                    link(nc.vector.tensor_scalar(crowded[:, :], most, float(P), None, ALU.is_gt))
                    signal(s_crowd)
                    signal(s_ppv)
                    signal(s_ppv)
                    full = dve.value_load(crowded[0:1, 0:1], min_val=0, max_val=1)
                    start = Tally(n)
                    with dve.If(full > 0):
                        ffn(N_EXPERTS)
                        residual()
                    n.clear()
                    n.update(start)
                    with dve.If(full < 1):
                        ffn(N_EXPERTS, sparse=True)
                        residual(True)
                else:
                    ffn(1)
                    residual()
                layer_norm(i + 1 < N_LAYERS)

            for l in range(N_LAYERS):
                n["layer"] = l

                def pre():
                    wait_rstd()
                    slot = gain()
                    for tt in range(TT):
                        link(nc.vector.scalar_tensor_tensor(out=t[:, tt, :], in0=x[:, tt, :], scalar=rstd[:, tt:tt + 1],
                                                            in1=vec[:, slot, :], op0=ALU.mult, op1=ALU.mult))
                        signal(s_rows)
                    signal(s_vecused)
                    lo_groups(uT_hi, uT_lo, 2)

                def post():
                    n["acc"] += 1
                    wait_rstd()
                    slot = gain()
                    for tt in range(TT):
                        o = t[:, tt, :]
                        link(nc.vector.scalar_tensor_tensor(out=o.rearrange("p (h c) -> p h c", h=2),
                                                            in0=acc[:, 2 * tt:2 * tt + 2, :],
                                                            scalar=rstd[:, tt:tt + 1],
                                                            in1=vec[:, slot, :].rearrange("p (h c) -> p h c", h=2),
                                                            op0=ALU.mult, op1=ALU.mult))
                        link(nc.vector.tensor_tensor(x[:, tt, :], x[:, tt, :], o, ALU.add))
                    signal(s_vecused)
                    signal(s_accfree)
                    signal(s_x)

                pre()
                dve.wait_ge(s_lam, 80 * (l + 1))
                for k in range(2):
                    link(nc.vector.tensor_tensor(lam4[:, 2 * k, :], lam4[:, 2 * k, :], lam4[:, 2 * k + 1, :],
                                                 ALU.mult))
                    link(nc.vector.tensor_reduce(lam_s[:, k:k + 1], lam4[:, 2 * k, :], AX_X, ALU.add))
                link(nc.vector.tensor_scalar(nsink, sink[:, :], -1.0, None, ALU.mult))
                signal(s_lamv)
                ffn(1)
                dve.wait_ge(s_lame, l + 1)
                lam_init = 0.8 - 0.6 * math.exp(-0.3 * l)
                link(nc.vector.tensor_tensor(nlam, lam_e[:, 1:2], lam_e[:, 0:1], ALU.subtract))
                link(nc.vector.tensor_scalar(nlam, nlam, -lam_init, None, ALU.add))
                post()
                pre()
                for br, (kind, cols) in enumerate((("na", ((0, 512), (512, 512), (1024, 512))),
                                                   ("sw", ((0, 512), (512, 256))),
                                                   ("diff", ((0, 512), (512, 512), (1024, 512))))):
                    for c0, width in cols:
                        turn = {"na": None, "sw": ((0, 8), (8, 10)), "diff": (None, (0, 16), None)}[kind]
                        turn = turn and turn[c0 // 512]
                        project_copy(c0, width, not turn)
                        n["ppa"] += 2
                        if turn:
                            dve.wait_ge(s_ppa, n["ppa"])
                            dve.wait_ge(s_ppv, n["pp"])
                            rotate(*turn, kind == "sw" and c0 == 0)
                            if c0 == 512:
                                signal(s_rows)
                            lo_chunk_a()
                    n["g"] += 4
                    attention(kind, 8, rows[:, :, 0:512], 512)
                    if kind == "diff":
                        o = rows[:, :, 0:512]
                        link(nc.vector.tensor_tensor(t[:, :, 0:512], o, o, ALU.mult))
                        link(nc.vector.tensor_reduce(ss[:, :].rearrange("p (t h) -> p t h", t=TT),
                                                     t[:, :, 0:512].rearrange("p t (h d) -> p t h d", h=4),
                                                     AX_X, ALU.add))
                        signal(s_sum)
                        wait_rstd()
                        slot = gain()
                        for tt in range(TT):
                            v = rows[:, tt, 0:512].rearrange("p (h d) -> p h d", h=4)
                            link(nc.vector.tensor_tensor(v, v, rstd[:, 4 * tt:4 * tt + 4].unsqueeze(2)
                                                         .to_broadcast([P, 4, 128]), ALU.mult))
                            link(nc.vector.tensor_tensor(v, v, vec[:, slot, 0:128].unsqueeze(1)
                                                         .to_broadcast([P, 4, 128]), ALU.mult))
                        signal(s_vecused)
                    for tt in range(TT):
                        signal(s_rows)
                    slot = gain()
                    for j in range(2):
                        for tt in range(TT):
                            n["pp"] += 1
                            dve.wait_ge(s_pp, n["pp"])
                            link(nc.vector.tensor_tensor(rows[:, tt, 1536 + 512 * j:2048 + 512 * j], pp[:, tt, :],
                                                         vec[:, slot, 512 * j:512 * (j + 1)], ALU.add))
                            signal(s_ppv)
                        signal(s_gl)
                        n["ppa"] += 2
                        lo_chunk_a()
                        if j == 0:
                            lo_groups(hT_hi, hT_lo, 1)
                    signal(s_vecused)
                    n["acc"] += 1
                    dve.wait_ge(s_acc, n["acc"])
                    dve.wait_ge(s_ppa, n["ppa"])
                    for tt in range(TT):
                        gate = rows[:, tt, 1536:2560].rearrange("p (h c) -> p h c", h=2)
                        o = (merged if br == 0 else t)[:, tt, :].rearrange("p (h c) -> p h c", h=2)
                        link(nc.vector.tensor_tensor(o, gate, acc[:, 2 * tt:2 * tt + 2, :], ALU.mult))
                        if br:
                            link(nc.vector.tensor_tensor(merged[:, tt, :], merged[:, tt, :], t[:, tt, :], ALU.add))
                        if br == 2:
                            signal(s_rows)
                    signal(s_accfree)
                    lo_chunk_a()
                lo_groups(uT_hi, uT_lo, 2)
                lo_chunk_a()
                post()
                pre()
                lo_chunk_a()
                ffn(1, l + 1 == N_LAYERS)
                post()

        @block.gpsimd
        def _(g):
            n = Tally()

            def link(ins):
                n["pool"] += 1
                ins.then_inc(s_pool, 1)
                g.wait_ge(s_pool, n["pool"])

            def load_gain():
                k = n["vec"]
                if k < len(GAINS):
                    if k >= 2:
                        g.wait_ge(s_vecused, k - 1)
                    src = GAINS[k]
                    w = src.shape[0]
                    g.dma_start(vec[:, k % 2, 0:w], row_bcast(src)).then_inc(s_vec[k % 2], 16)
                    n["vec"] += 1

            def deviations(parts, factor=1.0):
                for c0, c1, width, eps in parts:
                    link(nc.gpsimd.tensor_scalar(ss[:, c0:c1], ss[:, c0:c1], 1.0 / (width * factor ** 2),
                                                 eps / factor ** 2, ALU.mult, ALU.add))
                c1 = parts[-1][1]
                nc.gpsimd.tensor_tensor(rstd[:, 0:c1], ss[:, 0:c1], half_pow[:, 0:c1], ALU.pow).then_inc(s_rstd, 1)

            def rms(count, parts, factor=1.0):
                n["ss"] += count
                g.wait_ge(s_ss, n["ss"])
                deviations(parts, factor)

            def load_mask(which):
                if n["maskused"]:
                    g.wait_ge(s_maskused, n["maskused"])
                g.dma_start(mask[:, :, :], a["c_masks"][which].rearrange("(t p) k -> p t k", p=P)).then_inc(s_mask, 16)
                n["mask"] += 1

            def biases(load, heads, masked=True):
                g.wait_ge(s_mask, 16 * n["mask"])

                def start(h):
                    if n["bl"] >= 2:
                        g.wait_ge(s_biasused, n["bl"] - 1)
                    load(h, n["bl"] % 2)
                    n["bl"] += 1

                start(0)
                for h in range(heads):
                    if h + 1 < heads:
                        start(h + 1)
                    k = n["bias"]
                    n["landed%d" % (k % 2)] += 16
                    g.wait_ge(s_biasl[k % 2], n["landed%d" % (k % 2)])
                    if masked:
                        nc.gpsimd.tensor_tensor(bias[:, k % 2, :, :], bias[:, k % 2, :, :], mask[:, :, :], ALU.add) \
                          .then_inc(s_bias, 1)
                    else:
                        g.sem_inc(s_bias, 1)
                    n["bias"] += 1

            def layer_norm():
                n["sum"] += 1
                g.wait_ge(s_sum, n["sum"])
                nc.gpsimd.tensor_scalar(nmean, sm, -1.0 / D, None, ALU.mult).then_inc(s_nmean, 1)
                rms(2, [(0, 2, D, LN_EPS)])
                load_gain()
                load_gain()

            def store_bias(h):
                slot = h % 2
                g.wait_ge(s_nbld[slot], 64 * (n["nb_n%d" % slot] + 1))
                n["nb_n%d" % slot] += 1
                link(nc.gpsimd.tensor_tensor(bias[:, slot, :, :], bias[:, slot, :, :], mask[:, :, :], ALU.add))
                g.dma_start(na_bias[h].rearrange("(t p) k -> p t k", p=P), bias[:, slot, :, :]) \
                 .then_inc(s_nbst[slot], 16)

            g.dma_start(rows[0:12, 0, 127:384], a["rel_bias"].rearrange("l h r -> (l h) r")).then_inc(s_ext, 16)
            g.dma_start(rows[0:112, 1, 48:79], a["rpb_rows"]).then_inc(s_ext, 16)
            g.dma_start(rope[:, :, :, :], a["c_rope"].rearrange("c (t p) d -> p c t d", p=P)).then_inc(s_const, 16)
            g.dma_start(earlier[:, :], a["c_earlier"]).then_inc(s_const, 16)
            g.dma_start(rt[:, :].rearrange("p (k e) -> p k e", k=KD),
                        a["moe_router"][0].rearrange("(k p) e -> p k e", p=P)).then_inc(s_rt, 16)
            load_gain()
            load_gain()
            g.wait_ge(s_ext, 32)
            nc.gpsimd.tensor_copy(rows[0:12, 0, 0:127], rows[0:12, 0, 127:128].to_broadcast([12, 127]))
            nc.gpsimd.tensor_copy(rows[0:12, 0, 384:511], rows[0:12, 0, 383:384].to_broadcast([12, 127]))
            nc.gpsimd.tensor_copy(rows[0:112, 1, 0:48], rows[0:112, 1, 48:49].to_broadcast([112, 48]))
            link(nc.gpsimd.tensor_copy(rows[0:112, 1, 79:127], rows[0:112, 1, 78:79].to_broadcast([112, 48])))
            g.dma_start(ext1, rows[0:12, 0, 0:511]).then_inc(s_ext, 16)
            g.dma_start(ext2, rows[0:112, 1, 0:127]).then_inc(s_ext, 16)
            g.wait_ge(s_ext, 64)
            g.wait_ge(s_zero, 3)
            g.dma_start(merged[:, :, :].rearrange("p s (g t) -> p s g t", g=4),
                        a["c_pool"].rearrange("(s p) g t -> p s g t", p=P)).then_inc(s_pw, 16)

            for i in range(N_LAYERS):
                g.dma_start(pool_w[:, :, :], a["pool_w"][i].rearrange("g c d -> c g d")).then_inc(s_pw, 16)
                load_mask(0)

                def chunk_bias(h, slot):
                    src = bass.AP(ext1.tensor, (i * CHUNK_HEADS + h) * 511, [[1, P], [P, TT], [1, S]])
                    g.dma_start(bias[:, slot, :, :], src).then_inc(s_biasl[slot], 16)

                biases(chunk_bias, CHUNK_HEADS)
                load_gain()
                g.wait_ge(s_bias, n["bias"])
                load_mask(1)
                n["maskused"] += 1
                if i == 1:
                    g.wait_ge(s_maskused, n["maskused"])
                    for k, dst in enumerate((slot_ids, before_op, any_op)):
                        g.dma_start(dst, a["c_slots"][:, k * P:(k + 1) * P]).then_inc(s_slots, 16)
                rms(6, [(3 * tt + k, 3 * tt + k + 1, w, RMS_EPS) for tt in range(TT)
                        for k, w in enumerate((D_POOL, D_CHUNK, D_SB))])
                load_gain()
                layer_norm()
                layer_norm()
            for l in range(N_LAYERS):
                rms(2, [(0, 2, D, RMS_EPS)])
                load_gain()
                for k, name in enumerate(("q1", "k1", "q2", "k2")):
                    g.dma_start(lam4[:, k, :], row_bcast(a["diff_lambda_%s_2" % name][l])).then_inc(s_lam, 16)
                g.dma_start(sink[:, :], row_bcast(a["sw_sink_2"][l])).then_inc(s_lam, 16)
                load_mask(2)
                g.wait_ge(s_mask, 16 * n["mask"])
                for h in range(NA_HEADS):
                    slot = h % 2
                    if h >= 2:
                        n["nb_st%d" % slot] += 16
                        g.wait_ge(s_nbst[slot], n["nb_st%d" % slot])
                    for r in range(NA_ROWS):
                        src = bass.AP(ext2.tensor, ((l * NA_HEADS + h) * 7 + r) * 127,
                                      [[1, GRID_W], [127, NA_ROWS], [1, GRID_W]])
                        dst = bias[64 * (r % 2):64 * (r % 2) + 64, slot, r // 2, :]
                        g.dma_start(dst.rearrange("p (a b) -> p a b", a=NA_ROWS), src).then_inc(s_nbld[slot], 16)
                    n["nb_ld%d" % slot] += 64
                    if h >= 1:
                        store_bias(h - 1)
                store_bias(NA_HEADS - 1)
                for slot in range(2):
                    n["nb_st%d" % slot] += 16
                    g.wait_ge(s_nbst[slot], n["nb_st%d" % slot])
                load_mask(3)
                rms(2, [(0, 2, D, RMS_EPS)], 0.5)
                load_gain()
                rms(2, [(0, 2, D, RMS_EPS)])
                load_gain()

                def load_na(h, slot):
                    g.dma_start(bias[:, slot, :, :], na_bias[h].rearrange("(t p) k -> p t k", p=P)) \
                     .then_inc(s_biasl[slot], 16)

                biases(load_na, NA_HEADS, masked=False)
                n["maskused"] += 1
                load_gain()
                load_gain()
                n["sum"] += 1
                g.wait_ge(s_sum, n["sum"])
                lam_init = 0.8 - 0.6 * math.exp(-0.3 * l)
                deviations([(0, 8, 128, RMS_EPS)], 1.0 - lam_init)
                load_gain()
                load_gain()
                rms(2, [(0, 2, D, RMS_EPS)])
                load_gain()
                rms(2, [(0, 2, D, RMS_EPS)])
                load_gain()
                rms(2, [(0, 2, D, RMS_EPS)], 0.5)
                load_gain()


NAMES = ["x", "w_in", "pool_w", "pool_scale", "rel_bias", "g_mix", "w_out", "ln1_g", "ln1_b", "ln2_g", "ln2_b",
         "ffn_wg", "ffn_wu", "ffn_wd", "moe_router", "moe_wg", "moe_wu", "moe_wd", "ffn1_pre_g_2", "ffn1_w_gu_2",
         "ffn1_w_down_2", "ffn1_post_g_2", "mix_pre_g_2", "w_in_2", "sw_sink_2", "diff_lambda_q1_2",
         "diff_lambda_k1_2", "diff_lambda_q2_2", "diff_lambda_k2_2", "diff_subln_g_2", "w_branch_2", "b_gate_2",
         "w_out_2", "mix_post_g_2", "ffn2_pre_g_2", "ffn2_w_gu_2", "ffn2_w_down_2", "ffn2_post_g_2"]


def kernel(**inputs):
    import concourse.bacc as bacc
    from concourse.bass_utils import run_bass_kernel_spmd as run

    nc = bacc.Bacc("TRN2", target_bir_lowering=False, num_devices=1, dynamic_dma_scratch_size=2048)
    arrays = {name: np.ascontiguousarray(inputs[name]) for name in NAMES}
    arrays["rpb_rows"] = np.ascontiguousarray(np.asarray(inputs["na_rpb_2"])[:, :, 4:11, :][:, :, ::-1, ::-1]
                                              .reshape(N_LAYERS * NA_HEADS * 7, 31))
    arrays.update(shape_constants())
    aps = {}
    for name, v in arrays.items():
        aps[name] = nc.dram_tensor("in_" + name, v.shape, mybir.dt.from_np(v.dtype), kind="ExternalInput").ap()
    out = nc.dram_tensor("out_0", (1, S, D), F32, kind="ExternalOutput").ap()
    program(nc, aps, out)
    r = run(nc, [{"in_" + name: v for name, v in arrays.items()}], core_ids=[0])
    return r.results[0]["out_0"]
```
